# Optimizing a Trainium2 kernel written in Bass

```python
import math
import jax, jax.numpy as jnp
from jax import lax
import numpy as np

D_MODEL = 1024
BATCH = 1
SEQ = 256
DEPTH = 1

ATT_HEADS = 8
HEAD_DIM = 64
ATT_WIDTH = ATT_HEADS * HEAD_DIM
CONV_GROUPS = 8
CONV_WIDTH = D_MODEL - ATT_WIDTH
CONV_K = 3
FFN_CONV_K = 3
D_FF = 2816
Q_BLOCK = 128
RMS_EPS = 1e-6
IN_COLS = 3 * ATT_WIDTH + 3 * CONV_WIDTH + 2 * D_MODEL
IN_SPLITS = (ATT_WIDTH, 2 * ATT_WIDTH, 3 * ATT_WIDTH,
             3 * ATT_WIDTH + CONV_WIDTH, 3 * ATT_WIDTH + 2 * CONV_WIDTH,
             3 * ATT_WIDTH + 3 * CONV_WIDTH, 3 * ATT_WIDTH + 3 * CONV_WIDTH + D_MODEL)


def rms_norm(x, g):
    xf = x.astype(jnp.float32)
    var = jnp.mean(xf * xf, axis=-1, keepdims=True)
    return (xf * lax.rsqrt(var + RMS_EPS) * g.astype(jnp.float32)).astype(x.dtype)

def causal_dwconv(u, w):
    kw = w.shape[0]
    s = u.shape[1]
    up = jnp.pad(u, ((0, 0), (kw - 1, 0), (0, 0)))
    y = up[:, 0:s, :] * w[0]
    for i in range(1, kw):
        y = y + up[:, i:i + s, :] * w[i]
    return y

def stick_breaking_attention(q, k, v):
    _, _, s, dh = q.shape
    scale = 1.0 / math.sqrt(dh)
    outs = []
    for blk in range(s // Q_BLOCK):
        t0 = blk * Q_BLOCK
        t1 = t0 + Q_BLOCK
        qb = q[:, :, t0:t1]
        kb = k[:, :, :t1]
        vb = v[:, :, :t1]
        z = jnp.einsum("bhqd,bhkd->bhqk", qb, kb).astype(jnp.float32) * scale
        t_idx = t0 + jnp.arange(Q_BLOCK)[:, None]
        s_idx = jnp.arange(t1)[None, :]
        strict = s_idx < t_idx
        log_keep = jnp.where(strict, jax.nn.log_sigmoid(-z), 0.0)
        later = lax.cumsum(log_keep, axis=3, reverse=True) - log_keep
        w = jnp.where(strict, jnp.exp(jax.nn.log_sigmoid(z) + later), 0.0)
        outs.append(jnp.einsum("bhqk,bhkd->bhqd", w, vb.astype(jnp.float32)))
    return jnp.concatenate(outs, axis=2).astype(q.dtype)

def first_inputs(seed: int = 0) -> dict:
    key = jax.random.key(seed)
    ks = jax.random.split(key, 14)
    f32 = jnp.float32

    def nrm(k, shape, fan_in):
        return jax.random.normal(k, shape, f32) * (fan_in ** -0.5)

    def gain(k):
        return 1.0 + 0.05 * jax.random.normal(k, (DEPTH, D_MODEL), f32)

    return {
        "x": jax.random.normal(ks[0], (BATCH, SEQ, D_MODEL), f32),
        "norm_mix_pre": gain(ks[1]),
        "w_in": nrm(ks[2], (DEPTH, D_MODEL, IN_COLS), D_MODEL),
        "conv_mix_w": nrm(ks[3], (DEPTH, CONV_K, CONV_WIDTH), CONV_K),
        "w_att_branch": nrm(ks[4], (DEPTH, ATT_WIDTH, D_MODEL), ATT_WIDTH),
        "w_conv_branch": nrm(ks[5], (DEPTH, CONV_WIDTH, D_MODEL), CONV_WIDTH),
        "w_out": nrm(ks[6], (DEPTH, D_MODEL, D_MODEL), D_MODEL),
        "norm_mix_post": gain(ks[7]),
        "norm_ffn_pre": gain(ks[8]),
        "w_up": nrm(ks[9], (DEPTH, D_MODEL, 2 * D_FF), D_MODEL),
        "conv_ffn_w": nrm(ks[10], (DEPTH, FFN_CONV_K, 2 * D_FF), FFN_CONV_K),
        "w_down": nrm(ks[11], (DEPTH, D_FF, D_MODEL), D_FF),
        "norm_ffn_post": gain(ks[12]),
    }

def first_block(x, norm_mix_pre, w_in, conv_mix_w, w_att_branch, w_conv_branch, w_out,
              norm_mix_post, norm_ffn_pre, w_up, conv_ffn_w, w_down, norm_ffn_post):
    b, s, _ = x.shape
    for l in range(DEPTH):
        h = rms_norm(x, norm_mix_pre[l])
        proj = h @ w_in[l]
        q, k, v, cb, cc, cx, g_att, g_conv = jnp.split(proj, IN_SPLITS, axis=-1)

        def heads(t):
            return t.reshape(b, s, ATT_HEADS, HEAD_DIM).transpose(0, 2, 1, 3)

        o = stick_breaking_attention(heads(q), heads(k), heads(v))
        y_att = o.transpose(0, 2, 1, 3).reshape(b, s, ATT_WIDTH) @ w_att_branch[l]

        y_conv = (cb * causal_dwconv(cc * cx, conv_mix_w[l])) @ w_conv_branch[l]

        merged = jax.nn.sigmoid(g_att) * y_att + jax.nn.sigmoid(g_conv) * y_conv
        x = x + rms_norm(merged @ w_out[l], norm_mix_post[l])

        h = rms_norm(x, norm_ffn_pre[l])
        u = causal_dwconv(h @ w_up[l], conv_ffn_w[l])
        a, g = jnp.split(u, 2, axis=-1)
        f = (jax.nn.gelu(g, approximate=True) * a) @ w_down[l]
        x = x + rms_norm(f, norm_ffn_post[l])
    return x


GDN_HEADS = 8
GDN_DK = 128
GDN_DV = 128
GDN_CONV = 4
GDN_CHUNK = 64
FOX_HEADS = 8
FOX_DH = 128
FOX_BLOCK = 128
D_FF_2 = 4 * D_MODEL
EPS = 1e-6

GDN_QK_W = GDN_HEADS * GDN_DK
GDN_V_W = GDN_HEADS * GDN_DV
FOX_W = FOX_HEADS * FOX_DH
IN_SPLITS_2 = (GDN_QK_W, GDN_QK_W, GDN_V_W, GDN_V_W, GDN_HEADS, GDN_HEADS,
             FOX_W, FOX_W, FOX_W, FOX_HEADS, D_MODEL, D_MODEL)
N_IN = sum(IN_SPLITS_2)


def rmsnorm(x, g):
    xf = x.astype(jnp.float32)
    y = xf * lax.rsqrt(jnp.mean(xf * xf, axis=-1, keepdims=True) + EPS)
    return (y * g.astype(jnp.float32)).astype(x.dtype)

def l2norm(x):
    xf = x.astype(jnp.float32)
    return xf * lax.rsqrt(jnp.sum(xf * xf, axis=-1, keepdims=True) + EPS)

def to_heads(x, n_heads):
    b, t, w = x.shape
    return x.reshape(b, t, n_heads, w // n_heads).transpose(0, 2, 1, 3)

def causal_depthwise_conv(x, w):
    k_width = w.shape[0]
    t = x.shape[1]
    xp = jnp.pad(x, ((0, 0), (k_width - 1, 0), (0, 0)))
    y = xp[:, 0:t] * w[0]
    for i in range(1, k_width):
        y = y + xp[:, i:i + t] * w[i]
    return y

def gated_delta_rule_chunked(q, k, v, g, beta):
    b, h, t, dk = q.shape
    dv = v.shape[-1]
    c = GDN_CHUNK
    n = t // c
    q = q.reshape(b, h, n, c, dk)
    k = k.reshape(b, h, n, c, dk)
    v = v.reshape(b, h, n, c, dv)
    g = g.reshape(b, h, n, c)
    beta = beta.reshape(b, h, n, c)

    G = jnp.cumsum(g, axis=-1)
    diff = G[..., :, None] - G[..., None, :]
    tri_incl = jnp.tril(jnp.ones((c, c), dtype=bool))
    tri_strict = jnp.tril(jnp.ones((c, c), dtype=bool), -1)
    decay = jnp.where(tri_incl, jnp.exp(jnp.where(tri_incl, diff, 0.0)), 0.0)

    kk = jnp.einsum('bhncd,bhnsd->bhncs', k, k)
    a_mat = jnp.where(tri_strict, beta[..., None] * kk * decay, 0.0)
    eye = jnp.eye(c, dtype=jnp.float32)
    rhs = jnp.concatenate([v * beta[..., None], k * (beta * jnp.exp(G))[..., None]], axis=-1)
    a_full = jnp.broadcast_to(a_mat + eye, (b, h, n, c, c))
    sol = lax.linalg.triangular_solve(a_full, rhs, left_side=True, lower=True,
                                      unit_diagonal=True)
    value, k_cum = sol[..., :dv], sol[..., dv:]

    attn_intra = jnp.einsum('bhncd,bhnsd->bhncs', q, k) * decay
    q_dec = q * jnp.exp(G)[..., None]
    g_last = G[..., -1:]
    k_dec = k * jnp.exp(g_last - G)[..., None]
    chunk_decay = jnp.exp(g_last[..., 0])

    def step(s, inp):
        value_c, kcum_c, attn_c, qdec_c, kdec_c, dec_c = inp
        v_new = value_c - jnp.einsum('bhcd,bhde->bhce', kcum_c, s)
        o = (jnp.einsum('bhcd,bhde->bhce', qdec_c, s)
             + jnp.einsum('bhcs,bhse->bhce', attn_c, v_new))
        s = s * dec_c[..., None, None] + jnp.einsum('bhcd,bhce->bhde', kdec_c, v_new)
        return s, o

    xs = tuple(jnp.moveaxis(a, 2, 0) for a in (value, k_cum, attn_intra, q_dec, k_dec, chunk_decay))
    s0 = jnp.zeros((b, h, dk, dv), jnp.float32)
    _, o = lax.scan(step, s0, xs)
    return jnp.moveaxis(o, 0, 2).reshape(b, h, t, dv)

def forgetting_attention(q, k, v, log_f):
    t = q.shape[2]
    cum = jnp.cumsum(log_f, axis=-1)
    scale = FOX_DH ** -0.5
    outs = []
    for i in range(t // FOX_BLOCK):
        q0 = i * FOX_BLOCK
        q1 = q0 + FOX_BLOCK
        s = (jnp.einsum('bhqd,bhkd->bhqk', q[:, :, q0:q1], k[:, :, :q1]) * scale
             + cum[:, :, q0:q1, None] - cum[:, :, None, :q1])
        mask = (q0 + jnp.arange(FOX_BLOCK))[:, None] >= jnp.arange(q1)[None, :]
        p = jax.nn.softmax(jnp.where(mask, s, -jnp.inf), axis=-1)
        outs.append(jnp.einsum('bhqk,bhkd->bhqd', p, v[:, :, :q1]))
    return jnp.concatenate(outs, axis=2)

def second_inputs(seed: int = 0) -> dict:
    key = jax.random.key(seed)
    ks = jax.random.split(key, 20)
    f32 = jnp.float32

    def nrm(k, shape, fan_in):
        return jax.random.normal(k, shape, f32) * (fan_in ** -0.5)

    def gain(k, shape):
        return 1.0 + 0.02 * jax.random.normal(k, shape, f32)

    dt = jnp.exp(jax.random.uniform(ks[5], (DEPTH, GDN_HEADS), f32,
                                    minval=float(np.log(1e-3)), maxval=float(np.log(1e-1))))
    return {
        "x": jax.random.normal(ks[0], (BATCH, SEQ, D_MODEL), f32),
        "norm_mix_g": gain(ks[1], (DEPTH, D_MODEL)),
        "w_in": nrm(ks[2], (DEPTH, D_MODEL, N_IN), D_MODEL),
        "gdn_conv_w": nrm(ks[3], (DEPTH, GDN_CONV, 2 * GDN_QK_W + GDN_V_W), GDN_CONV),
        "gdn_a_log": jnp.log(jax.random.uniform(ks[4], (DEPTH, GDN_HEADS), f32, minval=1.0, maxval=16.0)),
        "gdn_dt_bias": dt + jnp.log(-jnp.expm1(-dt)),
        "gdn_norm_g": gain(ks[6], (DEPTH, GDN_DV)),
        "fox_q_norm_g": gain(ks[7], (DEPTH, FOX_DH)),
        "fox_k_norm_g": gain(ks[8], (DEPTH, FOX_DH)),
        "fox_f_bias": jax.random.uniform(ks[9], (DEPTH, FOX_HEADS), f32, minval=2.0, maxval=6.0),
        "w_proj_gdn": nrm(ks[10], (DEPTH, GDN_V_W, D_MODEL), GDN_V_W),
        "w_proj_fox": nrm(ks[11], (DEPTH, FOX_W, D_MODEL), FOX_W),
        "w_out": nrm(ks[12], (DEPTH, D_MODEL, D_MODEL), D_MODEL),
        "norm_mlp_g": gain(ks[13], (DEPTH, D_MODEL)),
        "w_up": nrm(ks[14], (DEPTH, D_MODEL, D_FF_2), D_MODEL),
        "w_down": nrm(ks[15], (DEPTH, D_FF_2, D_MODEL), D_FF_2),
    }

def second_block(x, norm_mix_g, w_in, gdn_conv_w, gdn_a_log, gdn_dt_bias, gdn_norm_g,
              fox_q_norm_g, fox_k_norm_g, fox_f_bias, w_proj_gdn, w_proj_fox, w_out,
              norm_mlp_g, w_up, w_down):
    f32 = jnp.float32
    b, t, _ = x.shape
    split_idx = [int(i) for i in np.cumsum(IN_SPLITS_2)[:-1]]
    for l in range(DEPTH):
        u = rmsnorm(x, norm_mix_g[l])
        proj = u @ w_in[l]
        (gq, gk, gv, gz, ga, gb, fq, fk, fv, ff, gate_a, gate_b) = jnp.split(proj, split_idx, axis=-1)

        qkv = jax.nn.silu(causal_depthwise_conv(jnp.concatenate([gq, gk, gv], axis=-1), gdn_conv_w[l]))
        cq, ck, cv = jnp.split(qkv, [GDN_QK_W, 2 * GDN_QK_W], axis=-1)
        qh = l2norm(to_heads(cq, GDN_HEADS)) * (GDN_DK ** -0.5)
        kh = l2norm(to_heads(ck, GDN_HEADS))
        vh = to_heads(cv, GDN_HEADS).astype(f32)
        beta = jax.nn.sigmoid(gb.astype(f32)).transpose(0, 2, 1)
        g = (-jnp.exp(gdn_a_log[l].astype(f32))
             * jax.nn.softplus(ga.astype(f32) + gdn_dt_bias[l].astype(f32))).transpose(0, 2, 1)
        o_a = gated_delta_rule_chunked(qh, kh, vh, g, beta).transpose(0, 2, 1, 3)
        z = gz.reshape(b, t, GDN_HEADS, GDN_DV).astype(f32)
        o_a = rmsnorm(o_a, gdn_norm_g[l]) * jax.nn.silu(z)
        y_a = o_a.reshape(b, t, GDN_V_W).astype(x.dtype) @ w_proj_gdn[l]

        fqh = rmsnorm(to_heads(fq, FOX_HEADS), fox_q_norm_g[l]).astype(f32)
        fkh = rmsnorm(to_heads(fk, FOX_HEADS), fox_k_norm_g[l]).astype(f32)
        fvh = to_heads(fv, FOX_HEADS).astype(f32)
        log_f = jax.nn.log_sigmoid(ff.astype(f32) + fox_f_bias[l].astype(f32)).transpose(0, 2, 1)
        o_b = forgetting_attention(fqh, fkh, fvh, log_f).transpose(0, 2, 1, 3)
        y_b = o_b.reshape(b, t, FOX_W).astype(x.dtype) @ w_proj_fox[l]

        merged = jax.nn.sigmoid(gate_a) * y_a + jax.nn.sigmoid(gate_b) * y_b
        h = x + merged @ w_out[l]

        hn = rmsnorm(h, norm_mlp_g[l])
        x = h + jnp.square(jax.nn.relu(hn @ w_up[l])) @ w_down[l]
    return x


def setup_inputs(seed=0):
    out = dict(first_inputs(seed))
    for name, value in second_inputs(seed + 1).items():
        if name != "x":
            out[name + "_2"] = value
    return out


def reference(
    x, norm_mix_pre, w_in, conv_mix_w, w_att_branch, w_conv_branch, w_out, norm_mix_post,
    norm_ffn_pre, w_up, conv_ffn_w, w_down, norm_ffn_post, norm_mix_g_2, w_in_2, gdn_conv_w_2,
    gdn_a_log_2, gdn_dt_bias_2, gdn_norm_g_2, fox_q_norm_g_2, fox_k_norm_g_2, fox_f_bias_2,
    w_proj_gdn_2, w_proj_fox_2, w_out_2, norm_mlp_g_2, w_up_2, w_down_2,
):
    x = first_block(
        x, norm_mix_pre, w_in, conv_mix_w, w_att_branch, w_conv_branch, w_out, norm_mix_post,
        norm_ffn_pre, w_up, conv_ffn_w, w_down, norm_ffn_post,
    )
    return second_block(
        x, norm_mix_g_2, w_in_2, gdn_conv_w_2, gdn_a_log_2, gdn_dt_bias_2, gdn_norm_g_2,
        fox_q_norm_g_2, fox_k_norm_g_2, fox_f_bias_2, w_proj_gdn_2, w_proj_fox_2, w_out_2,
        norm_mlp_g_2, w_up_2, w_down_2,
    )


_drawn_inputs = setup_inputs


def setup_inputs(seed=0):
    import zlib

    import numpy as np

    out = dict(_drawn_inputs(seed))
    spreads = {}
    factors = {'norm_mix_g_2': 7.848,
     'gdn_norm_g_2': 8.0,
     'fox_q_norm_g_2': 21.394,
     'fox_k_norm_g_2': 8.0,
     'norm_mlp_g_2': 16.811}
    for name, (base, spread) in spreads.items():
        noise = np.random.default_rng([zlib.crc32(name.encode()), seed]).standard_normal(out[name].shape)
        drawn = base * np.exp(spread * noise) if base else spread * noise
        out[name] = __import__('jax').numpy.asarray(drawn.astype(out[name].dtype))
    for name, factor in factors.items():
        out[name] = (out[name] * factor).astype(out[name].dtype)
    return out
```

```python
from contextlib import ExitStack

import concourse.bass as bass
from concourse import mybir

F32 = mybir.dt.float32
F32R = mybir.dt.float32r
ALU = mybir.AluOpType
ACT = mybir.ActivationFunctionType
AX = mybir.AxisListType.X

P = 128
T = 256
D = 1024
DC = D // P
NH = 8
DFF1 = 2816
FC1 = DFF1 // P
DFF2 = 4096
FC2 = DFF2 // P
NEG = -1e30
KB = 1024
NRAW = 3
NW = 3
AHEAD = 2
MAIN = 3


class Queue:

    def __init__(self, sem, in_turn=False):
        self.sem, self.n, self.seen, self.prog, self.in_turn = sem, 0, {}, [], in_turn

    def wait(self, toks):
        for t in toks:
            if not t:
                continue
            if isinstance(t, list) or not isinstance(t[1], int):
                self.wait(t)
                continue
            sem, v = t
            if self.seen.get(sem.name, 0) < v:
                self.seen[sem.name] = v
                self.prog.append(lambda e, s=sem, v=v: e.wait_ge(s, v))

    def do(self, fn, *toks, sig=True):
        self.wait(toks)
        if self.in_turn and self.n:
            self.wait([self.now()])
        if not sig:
            self.prog.append(fn)
            return None
        self.n += 1
        self.prog.append(lambda e, s=self.sem: fn(e).then_inc(s, 1))
        return (self.sem, self.n)

    def now(self):
        return (self.sem, self.n)

    def play(self, e):
        for f in self.prog:
            f(e)


def two_blocks(nc, x, norm_mix_pre, w_in, conv_mix_w, w_att_branch, w_conv_branch, w_out, norm_mix_post,
               norm_ffn_pre, w_up, conv_ffn_w, w_down, norm_ffn_post, norm_mix_g_2, w_in_2, gdn_conv_w_2,
               gdn_a_log_2, gdn_dt_bias_2, gdn_norm_g_2, fox_q_norm_g_2, fox_k_norm_g_2, fox_f_bias_2,
               w_proj_gdn_2, w_proj_fox_2, w_out_2, norm_mlp_g_2, w_up_2, w_down_2, out):
    ctx = ExitStack()
    with ctx:
        base = 16640
        off = {"p": 0}

        def at(name, shape, o, dt=F32):
            return nc.alloc_sbuf_tensor_at(name, list(shape), dt, offset=base + int(o))

        def fixed(name, shape, dt=F32):
            n = 4
            for s in shape[1:]:
                n *= s
            t = at(name, shape, off["p"], dt)
            off["p"] += (n + 31) // 32 * 32
            return t

        def sem(name):
            return ctx.enter_context(nc.semaphore(name))

        RAW = [fixed(f"raw{i}", [P, 8, 256]) for i in range(NRAW)]
        WH = [fixed(f"wh{i}", [P, 8, 256], F32R) for i in range(NW)]
        WL = [fixed(f"wl{i}", [P, 8, 256], F32R) for i in range(NW)]
        XH = fixed("xh", [P, 8, T], F32R)
        XL = fixed("xl", [P, 8, T], F32R)
        XRES = fixed("xres", [P, 2, D])
        XS = fixed("xs", [P, 2, D])
        FG = fixed("fg", [P, 2, D])
        GP = fixed("gp", [P, D])
        ident = fixed("ident", [P, P])
        ones = fixed("ones", [P, P])
        TRI = fixed("tri", [P, P])
        UF = fixed("uf", [P, P])
        UI = fixed("ui", [P, P])
        UL = fixed("ul", [P, P])
        USM = fixed("usm", [P, P])
        ONEB = fixed("oneb", [P, 2, P])
        MK3 = fixed("mk3", [P, 384])
        ML = fixed("ml", [P, 5, P])
        M1T = fixed("m1t", [P, P])
        COLS = fixed("cols", [P, 276])
        ss = fixed("ss", [P, 4])
        rs = fixed("rs", [P, 4])
        npow = fixed("npow", [P, 16])
        ppow = fixed("ppow", [P, 4])
        hb = fixed("hb", [P, 3, 8])
        gsm = fixed("gsm", [P, 2, 24])
        gv_ = fixed("gv_", [P, 12, 2, 8])
        DEC = fixed("dec", [P, 4, 8])
        CG = {"mix": 0, "ffn": 8, "mix2": 16, "mlp2": 24, "cmix": 32, "gn": 44, "fq": 45, "fk": 46,
              "cfa": 47, "cfg": 113, "gdn": 179}
        R0 = off["p"]
        assert base + R0 + 80 * KB <= nc.sbuf_usable_end, (base + R0 + 80 * KB, nc.sbuf_usable_end)

        def reg(name, shape, kb, dt=F32):
            return at(name, shape, R0 + kb * KB, dt)

        PS = [ctx.enter_context(nc.psum_tensor(f"ps{i}", [P, 512], F32)) for i in range(8)]

        pe, act, dve, pool, sp = (Queue(sem(f"s_{n}"), n == "pool") for n in ("pe", "act", "dve", "pool", "sp"))
        engines = (pe, act, dve, pool)

        later, side = [], []

        def defer(n, fn):
            later.append([n, fn])

        def run_later():
            while True:
                d = next((d for d in later if d[0] <= 0), None)
                if d is None:
                    return
                later.remove(d)
                d[1]()

        def flush():
            while later:
                m = min(d[0] for d in later)
                for d in later:
                    d[0] -= m
                run_later()

        def tick():
            for d in later:
                d[0] -= 1
            run_later()
            for g in list(side):
                if g in side and next(g, "end") == "end":
                    side.remove(g)

        def pause(n):
            for _ in range(n):
                yield

        def drain():
            while side:
                tick()
            flush()

        def fence():
            flush()
            return [q.now() for q in engines]

        def mm(o, l, r, start, stop, *toks, sig=False, loose=False):
            return pe.do(lambda e: e.matmul(o, l, r, start=start, stop=stop, skip_group_check=loose), *toks, sig=sig)

        def tr(o, i, *toks, sig=False):
            return pe.do(lambda e: e.transpose(o, i, ident[:]), *toks, sig=sig)

        def afn(o, i, f, *toks, **kw):
            return act.do(lambda e: e.activation(o, i, f, **kw), *toks)

        def tt(q, o, a, b, op, *toks):
            return q.do(lambda e: e.tensor_tensor(o, a, b, op), *toks)

        def ts(q, o, a, s1, s2, op0, op1, *toks):
            if op1 is None:
                return q.do(lambda e: e.tensor_scalar(o, a, s1, None, op0), *toks)
            return q.do(lambda e: e.tensor_scalar(o, a, s1, s2, op0, op1), *toks)

        def stt(o, a, s, b, op0, op1, *toks):
            return dve.do(lambda e: e.scalar_tensor_tensor(o, a, s, b, op0, op1), *toks)

        def mid(ap, n):
            return ap.unsqueeze(1).broadcast_to([ap.shape[0], n, ap.shape[1]])

        def last(ap, n):
            return ap.unsqueeze(2).broadcast_to([ap.shape[0], ap.shape[1], n])

        n_dma = [0]

        def load(q, dst, src):
            s = sem(f"ld{n_dma[0]}")
            n_dma[0] += 1
            q.prog.append(lambda e: e.dma_start(dst, src).then_inc(s, 16))
            return (s, 16)

        xv = x[0].rearrange("(a p) n -> p a n", p=P)
        x_in = [load(sp, XRES[:, a, :], xv[:, a, :]) for a in range(2)]
        R1 = reg("r1", [P, P], 76)
        R2 = reg("r2", [P, P], 76.5)
        R3 = reg("r3", [P, P], 77)
        R4 = reg("r4", [P, P], 77.5)
        rows = []

        def row(dst, src):
            rows.append(load(act, dst, src))

        chunks = "a (c p) -> (a c) p"
        row(R1[0:8, :], norm_mix_pre.rearrange(chunks, p=P))
        row(R1[8:16, :], norm_ffn_pre.rearrange(chunks, p=P))
        row(R1[16:24, :], norm_mix_g_2.rearrange(chunks, p=P))
        row(R1[24:32, :], norm_mlp_g_2.rearrange(chunks, p=P))
        row(R1[32:44, :], conv_mix_w[0].rearrange(chunks, p=P))
        row(R1[44:45, :], gdn_norm_g_2)
        row(R1[45:46, :], fox_q_norm_g_2)
        row(R1[46:47, :], fox_k_norm_g_2)
        for k in range(3):
            row(R2[22 * k:22 * k + 22, :], conv_ffn_w[0, k:k + 1, 0:DFF1].rearrange(chunks, p=P))
            row(R3[22 * k:22 * k + 22, :], conv_ffn_w[0, k:k + 1, DFF1:2 * DFF1].rearrange(chunks, p=P))
        row(R4[0:96, :], gdn_conv_w_2[0].rearrange(chunks, p=P))
        hb_in = [load(act, hb[:, i, :], v[0].partition_broadcast(P))
                 for i, v in enumerate((gdn_dt_bias_2, gdn_a_log_2, fox_f_bias_2))]

        def setm(ap, v, *toks):
            return pool.do(lambda e: e.memset(ap, v), *toks)

        def sel(ap, cmp, fill, base_, pattern, cm, *toks):
            return pool.do(lambda e: e.affine_select(out=ap, in_=ap, compare_op=cmp, fill=fill, base=base_,
                                                     pattern=pattern, channel_multiplier=cm), *toks)

        k = setm(ident[:], 0.0)
        c_id = sel(ident[:], ALU.not_equal, 1.0, 0, [[-1, P]], 1, k)
        c_np = setm(npow[:], -0.5)
        c_on = setm(ones[:], 1.0)
        k = setm(TRI[:], 1.0)
        c_tri = sel(TRI[:], ALU.is_ge, 0.0, 0, [[-1, P]], 1, k)
        late = []

        def late_constants():
            k = setm(UF[:], 1.0)
            late.append(sel(UF[:], ALU.is_ge, 0.0, 0, [[1, P]], -1, k))
            for m, cmp, b_, st, cm in ((UI, ALU.is_ge, 0, 1, -1), (USM, ALU.is_gt, 0, 1, -1), (UL, ALU.is_gt, 0, -1, 1)):
                k = setm(m[:], 1.0)
                k = sel(m[:], cmp, 0.0, b_, [[st, P]], cm, k)
                if cm < 0:
                    late.append(setm(m[0:64, 64:128], 0.0, k))
                else:
                    late.append(setm(m[64:128, 0:64], 0.0, k))
            k = setm(ONEB[:], 0.0)
            late.append(setm(ONEB[0:64, 0, :], 1.0, k))
            late.append(setm(ONEB[64:128, 1, :], 1.0, k))
            k = setm(MK3[:], 0.0)
            for b in (0, 256):
                late.append(sel(MK3[:, b:b + 128], ALU.is_ge, NEG, 0, [[-1, P]], 1, k))
            k = setm(ML[:], 0.0)
            for i, b in enumerate((2, 4, 8, 16, 32)):
                nb = P // (2 * b)
                v = ML[:, i, :].rearrange("p (n z b) -> p n z b", z=2, b=b)[:, :, 0, :]
                k2 = setm(v, -1.0, k)
                k2 = sel(v, ALU.is_ge, 0.0, -b, [[-2 * b, nb], [0, b]], 1, k2)
                late.append(sel(v, ALU.is_ge, 0.0, 2 * b - 1, [[2 * b, nb], [0, b]], -1, k2))
            k = setm(M1T[:], 0.0)
            v = M1T[:].rearrange("p (n z) -> p n z", z=2)[:, :, 1]
            late.append(sel(v, ALU.not_equal, -1.0, 0, [[-2, 64]], 1, k))
            late.append(setm(ppow[:], 0.5))

        raw_sem = [sem(f"rw{i}") for i in range(NRAW)]
        raw_cnt = [0] * NRAW
        raw_free = [[] for _ in range(NRAW)]
        w_free = [[] for _ in range(NW)]
        bank_free = {i: [] for i in range(8)}
        units = []
        state = {"load": 0, "prep": 0, "bank": 0}
        def do_load(i):
            u = units[i]
            s = i % NRAW
            sp.wait(raw_free[s])
            raw_cnt[s] += 16
            dst, src = RAW[s][:, 0:u["kc"], :], u["src"]
            sp.prog.append(lambda e: e.dma_start(dst, src).then_inc(raw_sem[s], 16))
            u["raw"] = (raw_sem[s], raw_cnt[s])

        def do_prep(i):
            u = units[i]
            s, w, kc = i % NRAW, i % NW, u["kc"]
            u["ready"] = []
            half = (kc + 1) // 2
            for a, b in ((0, half), (half, kc)):
                h = afn(WH[w][:, a:b, :], RAW[s][:, a:b, :], ACT.Copy, u["raw"], w_free[w])
                lo = tt(dve, WL[w][:, a:b, :], RAW[s][:, a:b, :], WH[w][:, a:b, :].bitcast(F32), ALU.subtract, h, w_free[w])
                u["ready"] += [(h, lo)] * (b - a)
            raw_free[s] = [lo]

        def unit(src, kc, mode, xh, xl, xtok, evac, k0=0, first=True, last_=True, before=None):
            units.append(dict(src=src, kc=kc, mode=mode, xh=xh, xl=xl, xtok=xtok, evac=evac, k0=k0, first=first,
                              last=last_, before=before))

        def run_units():
            for i, u in enumerate(units):
                while state["load"] < min(len(units), i + AHEAD + NRAW):
                    if state["load"] - state["prep"] >= NRAW:
                        break
                    do_load(state["load"])
                    state["load"] += 1
                while state["prep"] < min(len(units), i + AHEAD + 1):
                    if state["prep"] >= state["load"]:
                        do_load(state["load"])
                        state["load"] += 1
                    do_prep(state["prep"])
                    state["prep"] += 1
                    if state["load"] < len(units) and state["load"] - state["prep"] < NRAW:
                        do_load(state["load"])
                        state["load"] += 1
                if u["before"]:
                    u["before"]()
                w, kc, k0 = i % NW, u["kc"], u["k0"]
                bk = state["bank"] % MAIN
                if u["first"]:
                    pe.wait(bank_free[bk])
                whole = u["first"] and u["last"]
                tok = None
                for c in range(2):
                    o = PS[bk][:, c * 256:(c + 1) * 256]
                    for q in range(kc):
                        while u["xtok"](k0 + q) is None:
                            tick()
                        pe.wait([u["ready"][q], u["xtok"](k0 + q)])
                        xh, xl = u["xh"][:, k0 + q, :], u["xl"][:, k0 + q, :]
                        wh, wl = WH[w][:, q, :], WL[w][:, q, :]
                        if u["mode"] == "B":
                            wh, wl = wh[:, c * P:(c + 1) * P], wl[:, c * P:(c + 1) * P]
                            trio = ((wh, xh), (wh, xl), (wl, xh))
                        else:
                            xh, xl = xh[:, c * P:(c + 1) * P], xl[:, c * P:(c + 1) * P]
                            trio = ((xh, wh), (xh, wl), (xl, wh))
                        for j, (l, r) in enumerate(trio):
                            st = j == 0 and q == 0 and (u["first"] and (whole or c == 0))
                            end = j == 2 and q == kc - 1 and u["last"]
                            tok = mm(o, l, r, st, end, sig=(j == 2 and q == kc - 1), loose=not whole)
                        if q % 2:
                            tick()
                w_free[w] = [tok]
                if u["last"]:
                    bank_free[bk] = u["evac"](PS[bk], tok)
                    state["bank"] += 1

        xt_tok = [None] * 8
        xt_read = {"t": []}

        def norm_to_xt(gcol, xtoks, gtok=()):
            sc = [None, None]
            sq = [afn(XS[:, a, :], XRES[:, a, :], ACT.Square, xtoks[a], xs_free["t"], accum_out=ss[:, a:a + 1])
                  for a in range(2)]
            for a in range(2):
                k = ts(pool, rs[:, a:a + 1], ss[:, a:a + 1], 1.0 / D, 1e-6, ALU.mult, ALU.add, sq[a])
                k = tt(pool, rs[:, 2 + a:3 + a], rs[:, a:a + 1], npow[:, 0:1], ALU.pow, k, c_np)
                sc[a] = ts(dve, XS[:, a, :], XRES[:, a, :], rs[:, 2 + a:3 + a], None, ALU.mult, None, k, sq[a])
            free = xt_read["t"]
            turned = {}
            for a in range(2):
                for c in range(8):
                    b, j = 3 + c // 2, c % 2
                    t = tr(PS[b][:, j * 256 + a * P:j * 256 + (a + 1) * P], XS[:, a, c * P:(c + 1) * P],
                           sc[a], c_id, bank_free[b], sig=a == 1)
                    turned[c] = t
            for g in range(4):
                b = 3 + g
                hs = [afn(XH[:, c, :], PS[b][:, (c % 2) * 256:(c % 2 + 1) * 256], ACT.Identity, turned[2 * g + 1], free, gtok,
                          scale=COLS[:, gcol + c:gcol + c + 1]) for c in (2 * g, 2 * g + 1)]
                for c in (2 * g, 2 * g + 1):
                    lo = stt(XL[:, c, :], PS[b][:, (c % 2) * 256:(c % 2 + 1) * 256], COLS[:, gcol + c:gcol + c + 1],
                             XH[:, c, :].bitcast(F32), ALU.mult, ALU.subtract, hs, free)
                    xt_tok[c] = [hs[c % 2], lo]
                bank_free[b] = [lo]
            xs_free["t"] = [t]

        xs_free = {"t": []}

        def split(hi, lo, src, toks, free=(), q=None):
            h = afn(hi, src, ACT.Copy, list(toks), list(free))
            l = tt(q or dve, lo, src, hi.bitcast(F32), ALU.subtract, h, list(free))
            return [h, l]

        def split_later(hi, lo, src, toks, free, got):
            def first():
                h = afn(hi, src, ACT.Copy, list(toks), list(free))
                defer(2, lambda: got([h, tt(dve, lo, src, hi.bitcast(F32), ALU.subtract, h, list(free))]))
            defer(1, first)

        def w_cols(w, r0, kc, c0, n=256):
            return w[r0:r0 + kc * P, c0:c0 + n].rearrange("(k p) n -> p k n", p=P)

        def xt_of(q):
            return xt_tok[q]

        qT = reg("qT", [P, 4, T], 0)
        kT = reg("kT", [P, 4, T], 4)
        vS = reg("vS", [P, 2, 512], 8)
        ccs = [reg(f"ccs{i}", [P, 2, T], 12 + 2 * i) for i in range(2)]
        pp = reg("pp", [P, 2, T], 16)
        cvy = reg("cvy", [P, 2, T], 18)
        att = [[reg(f"at{n}{i}", [P, 384], 25 + 1.5 * (2 * n + i)) for i in range(2)] for n in range(4)]
        ycH = reg("ycH", [P, 4, T], 37, F32R)
        ycL = reg("ycL", [P, 4, T], 41, F32R)
        oH = reg("oH", [P, 4, T], 45, F32R)
        oL = reg("oL", [P, 4, T], 49, F32R)
        sga = reg("sga", [P, 8, T], 53)
        sgc = [reg(f"sgc{i}", [P, 2, T], 61 + 2 * i) for i in range(2)]
        mcv = reg("mcv", [P, 8, T], 65)
        mt = [reg(f"mt{i}", [P, 2, T], 73 + 2 * i) for i in range(2)]

        def gains():
            t = pe.do(lambda e: e.transpose(PS[7][:, 0:8], R1[0:8, :], ident[0:8, 0:8]), rows[0], c_id)
            k = dve.do(lambda e: e.tensor_copy(COLS[:, 0:8], PS[7][:, 0:8]), t)
            bank_free[7] = [k]
            return k

        def head_rows():
            yield
            t = bank_free[7]
            for src, n, c in ((R1, 47, 0), (R2, 66, 47), (R3, 66, 113), (R4, 96, 179)):
                t = pe.do(lambda e, src=src, n=n, c=c: e.transpose(PS[7][:, c:c + n], src[0:n, :], ident[0:n, 0:n]),
                          rows, t)
            yield
            t = dve.do(lambda e: e.tensor_copy(COLS[:, 8:275], PS[7][:, 8:275]), t)
            bank_free[7] = [t]
            tk["cols"] = t

        tk = {}
        act.prog.append(lambda e: e.preload_act_table_set("natural_log_exp_and_others"))
        norm_to_xt(CG["mix"], x_in, gains())
        side.append(head_rows())
        late_constants()

        w = w_in[0]
        A0, A1, A2 = 0, 512, 1024
        C0, C1, C2 = 1536, 2048, 2560
        GA, GC = 3072, 4096

        def keep(dst, key, i, scale=1.0):
            def evac(ps, t):
                k = act.do(lambda e: e.activation(dst[:, 2 * i:2 * i + 2, :].rearrange("p c t -> p (c t)"), ps[:],
                                                  ACT.Copy, scale=scale), t)
                tk[key, i] = k
                return [k]
            return evac

        for i in range(2):
            unit(w_cols(w, 0, 8, A0 + 256 * i), 8, "B", XH, XL, xt_of, keep(qT, "q", i, 0.125))
        for i in range(2):
            unit(w_cols(w, 0, 8, A1 + 256 * i), 8, "B", XH, XL, xt_of, keep(kT, "k", i))
        for i in range(2):
            def v_evac(ps, t, i=i):
                k = afn(vS[:, :, 256 * i:256 * i + 256], ps[:].rearrange("p (a n) -> p a n", a=2), ACT.Copy, t)
                tk["v", i] = k
                return [k]
            unit(w_cols(w, 0, 8, A2 + 256 * i), 8, "A", XH, XL, xt_of, v_evac)

        def cc_evac(ps, t):
            k = afn(ccs[0][:].rearrange("p c t -> p (c t)"), ps[:], ACT.Copy, t, tk.get("pp"))
            tk["cc"] = k
            return [k]

        def cx_evac(i):
            def evac(ps, t):
                c0 = CG["cmix"]
                k = tt(dve, pp[:].rearrange("p c t -> p (c t)"), ps[:], ccs[0][:].rearrange("p c t -> p (c t)"),
                       ALU.mult, t, tk["cc"], tk.get("cvy"))
                tk["pp"] = k

                def wc(j, n):
                    c = c0 + 4 * n + 2 * i + j
                    return COLS[:, c:c + 1]
                ys = [afn(cvy[:, j, :], pp[:, j, :], ACT.Identity, k, tk.get("yc"), tk["cols"], scale=wc(j, 2))
                      for j in range(2)]

                def rest():
                    tk["cvy"] = []
                    for j in range(2):
                        y = stt(cvy[:, j, 1:T], pp[:, j, 0:T - 1], wc(j, 1), cvy[:, j, 1:T], ALU.mult, ALU.add, ys[j])
                        y = stt(cvy[:, j, 2:T], pp[:, j, 0:T - 2], wc(j, 0), cvy[:, j, 2:T], ALU.mult, ALU.add, y)
                        tk["cvy"].append(y)
                    tk["pp"] = y
                defer(2, rest)
                return [k]
            return evac

        def cb_evac(i):
            def evac(ps, t):
                k = tt(dve, cvy[:].rearrange("p c t -> p (c t)"), ps[:], cvy[:].rearrange("p c t -> p (c t)"), ALU.mult,
                       t, tk["cvy"])

                def got(s):
                    tk["yc"] = s
                    tk["ycT", 2 * i] = tk["ycT", 2 * i + 1] = s
                split_later(ycH[:, 2 * i:2 * i + 2, :], ycL[:, 2 * i:2 * i + 2, :], cvy[:], [k], (), got)
                return [k]
            return evac

        def attention(e_):
            zs, e, s_, d = (att[n][e_] for n in range(4))
            bz, bc = 3 + 2 * e_, 4 + 2 * e_
            z, C = PS[bz], PS[bc]

            def diag(ap):
                return ap[:].rearrange("p (b t) -> p b t", b=3)[:, 0::2, :]

            k_o = None
            for h in range(e_, NH, 2):
                c, o = h // 2, 64 * e_
                kk, qq = kT[o:o + 64, c, :], qT[o:o + 64, c, :]
                while ("k", c // 2) not in tk:
                    yield
                mm(z[:, 0:256], kk[:, 0:P], qq, True, True, tk["q", c // 2], tk["k", c // 2], bank_free[bz])
                t = mm(z[:, 256:384], kk[:, P:T], qq[:, P:T], True, True, sig=True)
                yield
                z0 = afn(zs[:], z[:, 0:384], ACT.Copy, t)
                bank_free[bz] = [z0]
                a = afn(e[:], zs[:], ACT.Abs, z0)
                a = afn(e[:], e[:], ACT.Exp, a, scale=-1.0)
                a = afn(e[:], e[:], ACT.Ln, a, bias=1.0)
                yield from pause(5)
                k = stt(s_[:], zs[:], 0.0, e[:], ALU.max, ALU.add, a, z0)
                v = diag(s_)
                ks = pool.do(lambda en: en.affine_select(
                    out=v, in_=v, compare_op=ALU.is_gt, fill=0.0, base=0, pattern=[[0, 2], [1, P]],
                    channel_multiplier=-1), k)
                yield from pause(4)
                mm(C[:, 0:256], TRI[:], s_[:, 0:256], True, False, ks, c_tri, bank_free[bc], loose=True)
                mm(C[:, 128:256], ones[:], s_[:, 256:384], False, True, c_on, loose=True)
                t = mm(C[:, 256:384], TRI[:], s_[:, 256:384], True, True, sig=True, loose=True)
                yield
                k = tt(dve, d[:], zs[:], C[:, 0:384], ALU.subtract, t, z0, k_o)
                bank_free[bc] = [k]
                w_ = diag(d)
                k = pool.do(lambda en: en.affine_select(
                    out=w_, in_=w_, compare_op=ALU.is_gt, fill=NEG, base=0, pattern=[[0, 2], [1, P]],
                    channel_multiplier=-1), k)
                yield from pause(4)
                k = afn(d[:], d[:], ACT.Exp, k)
                yield from pause(2)
                while ("v", h // 4) not in tk:
                    yield
                mm(z[o:o + 64, 0:256], vS[:, 0, h * 64:(h + 1) * 64], d[:, 0:256], True, False, k, tk["v", h // 4],
                   bank_free[bz], loose=True)
                k_o = mm(z[o:o + 64, 128:256], vS[:, 1, h * 64:(h + 1) * 64], d[:, 256:384], False, True, sig=True,
                         loose=True)
                yield
                hh = afn(oH[o:o + 64, c, :], z[o:o + 64, 0:256], ACT.Copy, k_o)
                yield from pause(2)
                ll = tt(dve, oL[o:o + 64, c, :], z[o:o + 64, 0:256], oH[o:o + 64, c, :].bitcast(F32), ALU.subtract, hh)
                bank_free[bz] = [hh, ll]
                tk["oT", h] = [hh, ll]

        def start_attention():
            side.extend(attention(e_) for e_ in range(2))

        for i in range(2):
            unit(w_cols(w, 0, 8, C1 + 256 * i), 8, "B", XH, XL, xt_of, cc_evac,
                 before=start_attention if i == 0 else None)
            unit(w_cols(w, 0, 8, C2 + 256 * i), 8, "B", XH, XL, xt_of, cx_evac(i))
            unit(w_cols(w, 0, 8, C0 + 256 * i), 8, "B", XH, XL, xt_of, cb_evac(i))

        def gate_evac(dst, key, i, f=ACT.Sigmoid):
            def evac(ps, t):
                k = afn(dst, ps[:].rearrange("p (c t) -> p c t", c=2), f, t, tk.get(("free", key, i)))
                tk[key, i] = k
                return [k]
            return evac

        def yc_of(q):
            return tk.get(("ycT", q))

        def ycv_evac(i):
            def evac(ps, t):
                k = tt(dve, mcv[:, 2 * i:2 * i + 2, :].rearrange("p c t -> p (c t)"), ps[:],
                       sgc[i % 2][:].rearrange("p c t -> p (c t)"), ALU.mult, t, tk["gc", i])
                tk["free", "gc", i + 2] = k
                tk["mc", i] = k
                return [k]
            return evac

        for i in range(4):
            unit(w_cols(w, 0, 8, GC + 256 * i), 8, "B", XH, XL, xt_of, gate_evac(sgc[i % 2][:], "gc", i),
                 before=None)
            unit(w_cols(w_conv_branch[0], 0, 4, 256 * i), 4, "B", ycH, ycL, yc_of, ycv_evac(i))

        for i in range(4):
            unit(w_cols(w, 0, 8, GA + 256 * i), 8, "B", XH, XL, xt_of, gate_evac(sga[:, 2 * i:2 * i + 2, :], "ga", i))

        def o_of(q):
            if ("oT", 2 * q) in tk and ("oT", 2 * q + 1) in tk:
                return [tk["oT", 2 * q], tk["oT", 2 * q + 1]]
            return None

        m_tok = [None] * 8

        def yat_evac(i):
            def evac(ps, t):
                sl = slice(2 * i, 2 * i + 2)
                m = mt[i % 2]
                if i == 0:
                    xt_read["t"] = [tk["xt_done"]]
                k = tt(dve, m[:].rearrange("p c t -> p (c t)"), ps[:], sga[:, sl, :].rearrange("p c t -> p (c t)"),
                       ALU.mult, t, tk["ga", i], tk.get(("mt", i - 2)))
                k2 = tt(dve, m[:], m[:], mcv[:, sl, :], ALU.add, k, tk["mc", i])

                def got(s):
                    tk["mt", i] = s
                    m_tok[2 * i] = m_tok[2 * i + 1] = s
                split_later(XH[:, sl, :], XL[:, sl, :], m[:], [k2], xt_read["t"], got)
                return [k]
            return evac

        def y_att_start():
            tk["xt_done"] = pe.now()
            drain()

        for i in range(4):
            unit(w_cols(w_att_branch[0], 0, 4, 256 * i), 4, "B", oH, oL, o_of, yat_evac(i),
                 before=y_att_start if i == 0 else None)

        def m_of(q):
            return m_tok[q]

        def post_evac(i, key, gtok):
            def evac(ps, t):
                qs = []
                for a in range(2):
                    qs.append(afn(FG[:, a, 256 * i:256 * i + 256], ps[:, a * 256:(a + 1) * 256], ACT.Square, t,
                                  tk.get("fg_free"), accum_out=gv_[:, 11, a, i:i + 1]))
                g = GP[:, 256 * i:256 * i + 256]
                k = tt(dve, FG[:, :, 256 * i:256 * i + 256], ps[:].rearrange("p (a n) -> p a n", a=2), mid(g, 2), ALU.mult,
                       qs, tk[gtok])
                tk[key, i] = [qs, k]
                return [k]
            return evac

        def post_norm(key):
            al = [tk[key, i] for i in range(4)]
            r = [dve.do(lambda e, a=a: e.tensor_reduce(ss[:, a:a + 1], gv_[:, 11, a, 0:4], AX, ALU.add), al)
                 for a in range(2)]
            k = ts(pool, rs[:, 0:2], ss[:, 0:2], 1.0 / D, 1e-6, ALU.mult, ALU.add, r)
            k = tt(pool, rs[:, 2:4], rs[:, 0:2], npow[:, 0:2], ALU.pow, k)
            return [stt(XRES[:, a, :], FG[:, a, :], rs[:, 2 + a:3 + a], XRES[:, a, :], ALU.mult, ALU.add, k, al)
                    for a in range(2)]

        tk["g_post"] = load(sp, GP[:], norm_mix_post[0].partition_broadcast(P))
        for i in range(4):
            unit(w_cols(w_out[0], 0, 8, 256 * i), 8, "A", XH, XL, m_of, post_evac(i, "po", "g_post"))

        fH = reg("fH", [P, FC1, T], 0, F32R)
        fL = reg("fL", [P, FC1, T], 22, F32R)
        ya = [reg(f"ya{i}", [P, 2, T], 44 + 2 * i) for i in range(2)]
        yg = [reg(f"yg{i}", [P, 2, T], 48 + 2 * i) for i in range(2)]
        f_tok = [None] * FC2

        def second_norm():
            xt_read["t"] = [pe.now()]
            xs = post_norm("po")
            tk["g_post2"] = None
            k = fence()
            sp.wait(k)
            tk["g_post2"] = load(sp, GP[:], norm_ffn_post[0].partition_broadcast(P))
            norm_to_xt(CG["ffn"], xs)
            tk["fg_free"] = xs
            tk["ffn_f"] = fence()

        def conv_evac(dst, cbase, nch, taps, c0, key, fin):
            def evac(ps, t):
                ys = []
                for j in range(2):
                    def wc(n, c=c0 + j):
                        return COLS[:, cbase + nch * n + c:cbase + nch * n + c + 1]
                    ys.append(afn(dst[:, j, :], ps[:, j * 256:(j + 1) * 256], ACT.Identity, t, tk.get(("free", key)),
                                  tk.get("ffn_f"), scale=wc(taps - 1)))
                done = []
                for j in range(2):
                    def wc(n, c=c0 + j):
                        return COLS[:, cbase + nch * n + c:cbase + nch * n + c + 1]
                    y = ys
                    for d in range(1, taps):
                        y = stt(dst[:, j, d:T], ps[:, j * 256:j * 256 + T - d], wc(taps - 1 - d), dst[:, j, d:T], ALU.mult,
                                ALU.add, y)
                    done.append(y)
                fin(done)
                return [y]
            return evac

        for i in range(FC1 // 2):
            def fin_a(done, i=i):
                tk["ya", i] = done

            def fin_g(done, i=i):
                s = i % 2

                def got(r):
                    tk["free", "ya", i + 2] = r
                    f_tok[2 * i] = f_tok[2 * i + 1] = r

                def product():
                    k = afn(yg[s][:], yg[s][:], ACT.Gelu_apprx_tanh, done)
                    k = tt(pool, ya[s][:], ya[s][:], yg[s][:], ALU.mult, k, tk["ya", i])
                    tk["free", "yg", i + 2] = k
                    defer(3, lambda: split_later(fH[:, 2 * i:2 * i + 2, :], fL[:, 2 * i:2 * i + 2, :], ya[s][:], [k],
                                                 tk["ffn_f"], got))
                defer(2, product)

            unit(w_cols(w_up[0], 0, 8, 256 * i), 8, "B", XH, XL, xt_of,
                 (lambda ps, t, i=i, f=fin_a: conv_evac(ya[i % 2], CG["cfa"], FC1, 3, 2 * i, ("x", i), f)(ps, [t, tk.get(("free", "ya", i))])),
                 before=second_norm if i == 0 else None)
            unit(w_cols(w_up[0], 0, 8, DFF1 + 256 * i), 8, "B", XH, XL, xt_of,
                 (lambda ps, t, i=i, f=fin_g: conv_evac(yg[i % 2], CG["cfg"], FC1, 3, 2 * i, ("x", i), f)(ps, [t, tk.get(("free", "yg", i))])))

        def f_of(q):
            return f_tok[q]

        for i in range(4):
            for n, (r0, kc) in enumerate(((0, 8), (8, 8), (16, 6))):
                unit(w_cols(w_down[0], r0 * P, kc, 256 * i), kc, "A", fH, fL, f_of, post_evac(i, "po2", "g_post2"),
                     k0=r0, first=n == 0, last_=n == 2)

        gq = reg("gq", [P, 8, T], 0)
        gk = reg("gk", [P, 8, T], 8)
        gv = reg("gv", [P, 8, T], 16)
        fqm = reg("fqm", [P, 2, D], 24)
        fkm = reg("fkm", [P, 2, D], 32)
        fvm = reg("fvm", [P, 2, D], 40)
        fqT = XS[:].rearrange("p a (c t) -> p (a c) t", t=T)
        fkT = fqm[:].rearrange("p a (h d) -> p h a d", h=8)
        jk = [reg(f"jk{i}", [P, 512], 2 * i) for i in range(2)]
        sS = [reg(f"sS{i}", [P, 384], 48 + 1.5 * i) for i in range(2)]
        sT = [reg(f"sT{i}", [P, 384], 51 + 1.5 * i) for i in range(2)]
        CL = reg("CL", [64, T], 54)
        CX = reg("CX", [64, T], 55)
        CR = [reg(f"CR{i}", [64, T], 56 + i) for i in range(2)]
        stt2 = reg("stt2", [P, 8, 8], 58)
        HM = reg("HM", [64, 8], 58.5)
        gst = reg("gst", [24, T], 59)
        obH = reg("obH", [P, 8, T], 60, F32R)
        obL = reg("obL", [P, 8, T], 68, F32R)
        gsw = reg("gsw", [P, 8, 24], 76)
        gswH = reg("gswH", [P, 8, 24], 76.75, F32R)
        gswL = reg("gswL", [P, 8, 24], 77.5, F32R)
        E = FG
        Ev = E[:].rearrange("p a (h t) -> p a h t", h=8)
        (G_g, G_beta, G_G, G_os, G_eG, G_lf, G_dec, G_sq, G_sk, G_D, G_Dd, G_rt) = (gv_[:, i, :, :] for i in range(12))
        G_gl, G_fac = G_os, G_lf

        w2 = w_in_2[0]
        GQ, GK, GV, GZ, GSA = 0, 1024, 2048, 3072, 4096
        FQ, FK, FV, FFO = 4112, 5136, 6160, 7184
        GTA, GTB = 7192, 8216

        def third_norm():
            xt_read["t"] = [pe.now()]
            xs = post_norm("po2")
            norm_to_xt(CG["mix2"], xs)
            tk["fg_free"] = xs
            tk["b2"] = fence()
            sp.wait(tk["b2"])
            a = load(sp, gsw[:, :, 0:16], w2[:, GSA:GSA + 16].rearrange("(k p) n -> p k n", p=P))
            b = load(sp, gsw[:, :, 16:24], w2[:, FFO:FFO + 8].rearrange("(k p) n -> p k n", p=P))
            tk["gsw"] = split(gswH[:], gswL[:], gsw[:], [a, b], tk["b2"])
            act.prog.append(lambda e: e.preload_act_table_set("natural_log_exp_and_others"))
            side.append(small_side())

        def softplus(dst, src, tmp, toks, sign=1.0):
            a = afn(tmp, src, ACT.Abs, toks)
            a = afn(tmp, tmp, ACT.Exp, a, scale=-1.0)
            a = afn(tmp, tmp, ACT.Ln, a, bias=1.0)
            m = ts(dve, dst, src, sign, 0.0, ALU.mult, ALU.max, a)
            return tt(dve, dst, dst, tmp, ALU.add, m, a)

        def small_side():
            b = 3
            ps = PS[b]
            for q in range(8):
                xh, xl = XH[:, q, :], XL[:, q, :]
                for j, (l, r) in enumerate(((gswH[:, q, :], xh), (gswL[:, q, :], xh), (gswH[:, q, :], xl))):
                    t = mm(ps[0:24, 0:256], l, r, q == 0 and j == 0, q == 7 and j == 2, xt_tok[q], tk["gsw"],
                           bank_free[b], sig=q == 7 and j == 2)
            yield
            k = dve.do(lambda e: e.tensor_copy(gst[:], ps[0:24, 0:256]), t, tk["b2"])
            yield from pause(2)
            for a in range(2):
                t = pe.do(lambda e, a=a: e.transpose(ps[:, 256 + 24 * a:280 + 24 * a], gst[:, a * P:(a + 1) * P],
                                                     ident[0:24, 0:24]), k)
            yield
            k = dve.do(lambda e: e.tensor_copy(gsm[:], ps[:, 256:304].rearrange("p (a n) -> p a n", a=2)), t)
            bank_free[b] = [k]
            yield
            tmp = stt2[:, 0:2, :]
            x1 = tt(dve, G_g, gsm[:, :, 0:8], mid(hb[:, 0, :], 2), ALU.add, k, hb_in)
            s = softplus(G_G, G_g, tmp, [x1, tk["b2"]])
            ea = afn(hb[:, 1, :], hb[:, 1, :], ACT.Exp, hb_in)
            n = ts(dve, hb[:, 1, :], hb[:, 1, :], -1.0, None, ALU.mult, None, ea)
            g = tt(dve, G_g, G_G, mid(hb[:, 1, :], 2), ALU.mult, s, n)
            tmp2, tmp3 = stt2[:, 2:4, :], stt2[:, 4:6, :]
            s = softplus(tmp3, gsm[:, :, 8:16], tmp2, [k, tk["b2"]], -1.0)
            be = afn(G_beta, tmp3, ACT.Exp, s, scale=-1.0)
            x2 = tt(dve, gsm[:, :, 16:24], gsm[:, :, 16:24], mid(hb[:, 2, :], 2), ALU.add, k, hb_in)
            s = softplus(G_gl, gsm[:, :, 16:24], tmp2, [x2, be], -1.0)
            lf = ts(dve, G_lf, G_gl, -1.0, None, ALU.mult, None, s)
            yield
            b = 4
            ps4 = PS[b]
            mm(ps4[0:8, 0:128], G_lf[:, 0, :], UF[:], True, True, lf, late, bank_free[b], loose=True)
            mm(ps4[0:8, 128:256], G_lf[:, 0, :], ones[:], True, False, loose=True)
            mm(ps4[0:8, 128:256], G_lf[:, 1, :], UF[:], False, True, loose=True)
            mm(ps4[32:40, 0:128], G_lf[:, 0, :], UF[:], True, True, loose=True)
            mm(ps4[32:40, 128:256], G_lf[:, 0, :], ones[:], True, False, loose=True)
            t = mm(ps4[32:40, 128:256], G_lf[:, 1, :], UF[:], False, True, sig=True, loose=True)
            z = setm(CL[:], 0.0, tk["b2"])
            z = setm(CL[0:8, :], 1.0, z)
            z2 = setm(CX[:], 0.0, tk["b2"])
            z2 = setm(CX[32:64, :], 1.0, z2)
            m = setm(HM[:], 0.0, tk["b2"])
            m = sel(HM[0:32, :], ALU.not_equal, 1.0, 0, [[-1, 8]], 1, m)
            tk["HM"] = sel(HM[32:64, :], ALU.not_equal, 1.0, 0, [[-1, 8]], 1, m)
            c1 = dve.do(lambda e: e.tensor_copy(CL[32:40, :], ps4[32:40, 0:256]), t, z)
            c2 = ts(dve, CX[0:8, :], ps4[0:8, 0:256], -1.0, None, ALU.mult, None, t, z2)
            bank_free[b] = [c1, c2]
            tk["CL"], tk["CX"] = c1, c2
            yield
            b = 5
            ps5 = PS[b]
            pe.wait([g, late, bank_free[b]])
            gg = G_g.rearrange("p a h -> p (a h)")
            mm(ps5[:, 0:16], UI[:], gg, True, True, loose=True)
            mm(ps5[:, 16:32], UL[:], gg, True, True, loose=True)
            for c in range(2):
                t = mm(ps5[:, 32 + 16 * c:48 + 16 * c], ONEB[:, c, :], gg, True, True, sig=c == 1, loose=True)
            yield from pause(2)
            v2 = "p (a h) -> p a h"
            k = dve.do(lambda e: e.tensor_copy(G_G, ps5[:, 0:16].rearrange(v2, a=2)), t, g)
            k1 = afn(G_dec, ps5[:, 16:32].rearrange(v2, a=2), ACT.Exp, k)
            k2 = afn(DEC[:].rearrange("p (a c) h -> p c a h", c=2), ps5[:, 32:64].rearrange("p (c a h) -> p c a h", c=2, a=2),
                     ACT.Exp, tk["b2"])
            k0 = afn(G_eG, G_G, ACT.Exp, k)
            bank_free[b] = [k2]
            tk["Gs"] = [k, k0, k1, k2]
            yield from pause(2)
            for a in range(2):
                for h4 in range(2):
                    b = 3 + (2 * a + h4) % 2
                    for j in range(4):
                        h = 4 * h4 + j
                        gcol = G_g[:, a, h:h + 1].broadcast_to([P, P])
                        t = mm(PS[b][:, j * P:(j + 1) * P], gcol, UI[:], True, True, bank_free[b], sig=j == 3)
                    yield
                    for j in range(4):
                        h = 4 * h4 + j
                        k = ts(dve, Ev[:, a, h, :], PS[b][:, j * P:(j + 1) * P], G_G[:, a, h:h + 1], 0.0, ALU.subtract,
                               ALU.min, t, tk["Gs"], tk["fg_free"])
                    bank_free[b] = [k]
                    v = Ev[:, a, 4 * h4:4 * h4 + 4, :]
                    k = afn(v, v, ACT.Exp, k)
                    tk["E", a, h4] = tt(pool, v, v, mid(UI[:], 4), ALU.mult, k)
                    yield from pause(2)
            tk["E_all"] = tk["small"] = True

        def bcast(col2, bank, toks):
            for a in range(2):
                t = mm(PS[bank][:, a * P:(a + 1) * P], col2(a).broadcast_to([P, P]), ident[:], True, True, toks,
                       bank_free[bank], sig=a == 1)
            return t

        def fox_norm(key, i, tm, dst, k, sums, rstd, post):
            b = 6 + i % 2
            v = tm[:, :, 256 * i:256 * i + 256].rearrange("p a (j d) -> p a j d", j=2)
            js = jk[i % 2][:].rearrange("p (a j d) -> p a j d", a=2, j=2)
            hs = slice(2 * i, 2 * i + 2)
            k1 = afn(js, v, ACT.Square, k, tk["b2"], tk.get(("jk", i % 2)))
            yield from pause(2)
            r = dve.do(lambda e: e.tensor_reduce(sums[:, :, hs], js, AX, ALU.add), k1)
            tk["jk", i % 2] = r
            r = ts(pool, sums[:, :, hs], sums[:, :, hs], 1.0 / 128, 1e-6, ALU.mult, ALU.add, r)
            r = tt(pool, rstd[:, :, hs], sums[:, :, hs], npow[:, 0:4].rearrange("p (a h) -> p a h", a=2), ALU.pow, r)
            if post != 1.0:
                r = ts(pool, rstd[:, :, hs], rstd[:, :, hs], post, None, ALU.mult, None, r)
            yield from pause(5)
            r = [tt(dve, v[:, a], v[:, a], last(rstd[:, a, hs], P), ALU.mult, r, k1) for a in range(2)]
            yield from pause(3)
            for j in range(2):
                for a in range(2):
                    t = tr(PS[b][:, (2 * j + a) * P:(2 * j + a + 1) * P], v[:, a, j, :], r, bank_free[b],
                           sig=j == 1 and a == 1)
            yield
            if key == "fk":
                while ("fq", 3) not in tk:
                    yield
            kk = afn(dst[:, hs], PS[b][:].rearrange("p (j a d) -> p j a d", j=2, a=2) if key == "fk" else
                     PS[b][:].rearrange("p (j t) -> p j t", j=2), ACT.Identity, t, tk.get(("fq", 3)) if key == "fk" else (),
                     scale=COLS[:, CG[key]:CG[key] + 1])
            bank_free[b] = [kk]
            tk[key, i] = [kk, t]

        def fqk_evac(tm, dst, key, i, sums, rstd, post):
            def evac(ps, t):
                k = afn(tm[:, :, 256 * i:256 * i + 256], ps[:].rearrange("p (a n) -> p a n", a=2), ACT.Copy, t, tk["b2"])
                side.append(fox_norm(key, i, tm, dst, k, sums, rstd, post))
                return [k]
            return evac

        fox_left = [2]

        def fox_attention(e_):
            b = 3 + e_
            S, s, sTe = PS[b], sS[e_], sT[e_]
            halves = ((0, 128), (128, 384))
            m0 = stt2[:, 6, 2 * e_:2 * e_ + 2]
            l0 = stt2[:, 7, 2 * e_:2 * e_ + 2]
            t_s = t_o = None
            while not all(("fk", n) in tk for n in range(4)) or "CX" not in tk or "small" not in tk:
                yield
            for h in range(e_, NH, 2):
                cr = tt(pool, CR[e_][:], CX[:], HM[:, h:h + 1].broadcast_to([64, T]), ALU.mult, tk["CX"], tk["HM"], t_s)
                yield from pause(2)
                pe.wait([tk["fq", h // 2], tk["fk", h // 2], bank_free[b], tk["CL"]])
                mm(S[:, 0:128], fqT[:, h, 0:128], fkT[:, h, 0, :], True, False, loose=True)
                mm(S[:, 0:128], CL[:, 0:128], CR[e_][:, 0:128], False, True, cr, loose=True)
                mm(S[:, 128:384].rearrange("p (a d) -> p a d", a=2), fqT[:, h, 128:256], fkT[:, h], True, False, loose=True)
                t_s = mm(S[:, 128:384], CL[:, 128:256], CR[e_][:], False, True, sig=True, loose=True)
                yield from pause(2)
                k = tt(dve, s[:], S[:, 0:384], MK3[:], ALU.add, t_s)
                rs_ = [dve.do(lambda e, n=n, u=u, v=v: e.tensor_reduce(m0[:, n:n + 1], s[:, u:v], AX, ALU.max, negate=True),
                              k) for n, (u, v) in enumerate(halves)]
                ks = [afn(s[:, u:v], s[:, u:v], ACT.Exp, rs_, bias=m0[:, n:n + 1], accum_out=l0[:, n:n + 1])
                      for n, (u, v) in enumerate(halves)]
                yield from pause(4)
                r = dve.do(lambda e: e.reciprocal(l0, l0), ks)
                ns = [ts(dve, s[:, u:v], s[:, u:v], l0[:, n:n + 1], None, ALU.mult, None, r)
                      for n, (u, v) in enumerate(halves)]
                yield from pause(2)
                for n in range(3):
                    t = tr(S[:, n * P:(n + 1) * P], s[:, n * P:(n + 1) * P], ns, k, sig=n == 2)
                yield
                k = afn(sTe[:], S[:, 0:384], ACT.Copy, t, t_o)
                yield from pause(2)
                while ("fv", h // 2) not in tk:
                    yield
                mm(S[:, 0:256], fvm[:, 0, h * P:(h + 1) * P], sTe[:, 0:256], True, False, k, tk["fv", h // 2], loose=True)
                t_o = mm(S[:, 128:256], fvm[:, 1, h * P:(h + 1) * P], sTe[:, 256:384], False, True, sig=True, loose=True)
                yield
                hh = afn(obH[:, h, :], S[:, 0:256], ACT.Copy, t_o, tk["b2"])
                yield from pause(2)
                ll = tt(dve, obL[:, h, :], S[:, 0:256], obH[:, h, :].bitcast(F32), ALU.subtract, hh, tk["b2"])
                bank_free[b] = [ll]
                tk["ob", h] = [hh, ll]
            fox_left[0] -= 1
            if fox_left[0] == 0:
                tk["fox"] = fence()

        for i in range(4):
            unit(w_cols(w2, 0, 8, FQ + 256 * i), 8, "A", XH, XL, xt_of,
                 fqk_evac(fqm, fqT, "fq", i, G_sq, G_D, 128 ** -0.5), before=third_norm if i == 0 else None)
        for i in range(4):
            unit(w_cols(w2, 0, 8, FK + 256 * i), 8, "A", XH, XL, xt_of,
                 fqk_evac(fkm, fkT, "fk", i, G_sk, G_Dd, 1.0))
        for i in range(4):
            def fv_evac(ps, t, i=i):
                k = afn(fvm[:, :, 256 * i:256 * i + 256], ps[:].rearrange("p (a n) -> p a n", a=2), ACT.Copy, t, tk["b2"])
                tk["fv", i] = k
                return [k]
            unit(w_cols(w2, 0, 8, FV + 256 * i), 8, "A", XH, XL, xt_of, fv_evac,
                 before=(lambda: side.extend(fox_attention(e_) for e_ in range(2))) if i == 0 else None)

        def conv4_evac(dst, n, i):
            sl = dst[:, 2 * i:2 * i + 2, :]

            def fin(done):
                tk["cv", n, i] = done
                if n and i == 3:
                    defer(3, silu_k_and_q if n == 1 else silu_v)
            return lambda ps, t: conv_evac(sl, CG["gdn"], 24, 4, 8 * (1, 0, 2)[n] + 2 * i, ("x", 0), fin)(
                ps, [t, tk["b2"], tk["jk", 0], tk["jk", 1]])

        def silu(dst, n):
            tk["silu", n] = afn(dst[:], dst[:], ACT.Silu, [tk["cv", n, i] for i in range(4)])

        def silu_k_and_q():
            silu(gk, 0)
            silu(gq, 1)
            side.append(q_decay())
            side.extend(prologue(a, g) for a in range(2) for g in range(2))

        def silu_v():
            silu(gv, 2)

        for n, dst in enumerate((gk, gq, gv)):
            for i in range(4):
                unit(w_cols(w2, 0, 8, (GK, GQ, GV)[n] + 256 * i), 8, "B", XH, XL, xt_of, conv4_evac(dst, n, i))

        kb = reg("kb", [P, 8, T], 24)
        qd = reg("qd", [P, 8, T], 32)
        tA = [[reg(f"tA{n}{i}", [P, 4, P], 40 + 2 * (3 * i + n)) for n in range(3)] for i in range(3)]
        GPv = GP[:].rearrange("p (n h t) -> p n h t", n=2, h=4)
        tA.append([reg("tA03", [P, 4, P], 58)[:], GPv[:, 0], GPv[:, 1]])
        gz = reg("gz", [P, 8, T], 60)
        sg2 = reg("sg2", [P, 8, T], 68)
        mb = XS
        mbv = mb[:].rearrange("p a (c t) -> p (a c) t", t=T)
        S0 = reg("S0", [P, 8, P], 40)
        S1 = reg("S1", [P, 8, P], 44)
        Sd = reg("Sd", [P, 8, P], 48)
        VN = reg("VN", [P, 8, P], 52)
        oS = FG
        oSv = oS[:].rearrange("p a (h d) -> p a h d", h=8)
        mH = reg("mH", [P, 8, T], 0, F32R)
        mL = reg("mL", [P, 8, T], 8, F32R)
        sgb = [reg(f"sgb{i}", [P, 2, T], 76 + 2 * i) for i in range(2)]
        tokP = {}
        chains_left = [4]

        def q_decay():
            f0 = fence()
            yield
            b = 7
            for h in range(NH):
                t = bcast(lambda a: G_eG[:, a, h:h + 1], b, tk["Gs"])
                yield from pause(2)
                r = tt(dve, qd[:, h, :], gq[:, h, :], PS[b][:, 0:256], ALU.mult, t, f0, tk["silu", 1])
                tokP["qd", h] = r
                bank_free[b] = [r]
                yield

        def prologue(a, g):
            hs = range(4 * g, 4 * g + 4)
            AT, Y, Tm = tA[2 * a + g]
            AT, Y, Tm = AT[:, :, :], Y[:, :, :], Tm[:, :, :]
            b = 3 + 2 * a + g
            B4 = PS[b][:].rearrange("p (h t) -> p h t", h=4)
            tk_ = slice(a * P, (a + 1) * P)
            hsl = slice(4 * g, 4 * g + 4)
            Eg = Ev[:, a, hsl, :]
            kbs, gqs, gks, gvs = (v[:, hsl, tk_] for v in (kb, gq, gk, gv))

            def each(f, *toks):
                for j, h in enumerate(hs):
                    t = f(PS[b][:, j * P:(j + 1) * P], j, h, *toks, sig=j == 3)
                return t

            def turn(src, *toks):
                return each(lambda o, j, h, *tt_, sig: tr(o, src(j, h), *tt_, sig=sig), *toks)

            def prod(l, r, *toks):
                return each(lambda o, j, h, *tt_, sig: mm(o, l(j, h), r(j, h), True, True, *tt_, sig=sig), *toks)

            while "fox" not in tk or "E_all" not in tk:
                yield
            f0 = [tk["fox"], tk["E", a, g], tk["Gs"]]
            yield from pause(3 * a + g)
            t = turn(lambda j, h: gk[:, h, tk_], tk["silu", 0], f0, bank_free[b])
            yield
            kC = act.do(lambda e: e.activation(kbs, B4, ACT.Copy), t, f0)
            kS = act.do(lambda e: e.activation(Tm, kbs, ACT.Square), kC)
            yield
            t = turn(lambda j, h: gq[:, h, tk_], tk["silu", 1], kC)
            yield
            kQ = act.do(lambda e: e.activation(Y, B4, ACT.Square), t)
            yield
            sk, D_, Dd, rt = (v[:, a, hsl] for v in (G_sk, G_D, G_Dd, G_rt))
            r1 = dve.do(lambda e: e.tensor_reduce(sk, Tm, AX, ALU.add), kS)
            k = ts(dve, sk, sk, 1e-6, None, ALU.add, None, r1)
            kr = tt(pool, rt, sk, ppow[:], ALU.pow, k, late)
            kD = dve.do(lambda e: e.reciprocal(D_, sk), k)
            kD = tt(dve, D_, D_, G_beta[:, a, hsl], ALU.mult, kD)
            kDd = tt(dve, Dd, D_, G_dec[:, a, hsl], ALU.mult, kD)
            kE = tt(pool, Eg, Eg, last(D_, P), ALU.mult, kD)
            t = prod(lambda j, h: gk[:, h, tk_], lambda j, h: gk[:, h, tk_], kQ)
            yield
            rq = dve.do(lambda e: e.tensor_reduce(G_sq[:, a, hsl], Y, AX, ALU.add), kQ)
            tokP["sq", a, g] = rq
            yield from pause(2)
            kA = tt(dve, AT, B4, Eg, ALU.mult, t, kE)
            kA2 = tt(pool, AT, AT, mid(USM[:], 4), ALU.mult, kA)
            kY = tt(pool, Y, AT, mid(M1T[:], 4), ALU.mult, kA2, rq)
            kY = tt(pool, Y, Y, mid(ident[:], 4), ALU.add, kY)
            yield
            t = prod(lambda j, h: gk[:, h, tk_], lambda j, h: gq[:, h, tk_], kA)
            yield from pause(2)
            while not all(("qd", h) in tokP for h in hs):
                yield
            kT_ = tt(dve, gqs, B4, Eg, ALU.mult, t, [tokP["qd", h] for h in hs])
            tokP["att", a, g] = kT_
            yield
            while ("silu", 2) not in tk:
                yield
            t = turn(lambda j, h: gv[:, h, tk_], kT_, tk["silu", 2])
            yield from pause(2)
            rv = tt(dve, gvs, B4, last(rt, P), ALU.mult, t, kr)
            yield
            for i in range(5):
                t = turn(lambda j, h: Y[:, j, :], kY, rv)
                yield
                kTm = act.do(lambda e: e.activation(Tm, B4, ACT.Copy), t, r1)
                yield
                t = prod(lambda j, h: AT[:, j, :], lambda j, h: Tm[:, j, :], kTm, kA2)
                yield
                kU = tt(dve, Tm, B4, mid(ML[:, i, :], 4), ALU.mult, t)
                yield
                tY = prod(lambda j, h: Tm[:, j, :], lambda j, h: Y[:, j, :], kU)
                yield
                kY = tt(dve, Y, Y, B4, ALU.add, tY)
                rv = kY
                yield
            kR = tt(dve, Tm, kbs, last(G_eG[:, a, hsl], P), ALU.mult, tY, kC)
            kd = tt(pool, kbs, kbs, last(Dd, P), ALU.mult, kDd, kR)
            tokP["kd", a, g] = kd
            t = prod(lambda j, h: Y[:, j, :], lambda j, h: gv[:, h, tk_], kY)
            yield
            kV = act.do(lambda e: e.activation(gvs, B4, ACT.Copy), t)
            yield
            t = prod(lambda j, h: Tm[:, j, :], lambda j, h: Y[:, j, :], kR, kV)
            yield
            kC = act.do(lambda e: e.activation(gks, B4, ACT.Copy), t)
            bank_free[b] = [kC]
            tokP["v", a, g], tokP["c", a, g] = kV, kC
            tokP["end", a, g] = [kV, kC, t, kd]
            chains_left[0] -= 1
            if chains_left[0] == 0:
                side.append(scan())

        def scan():
            ends = [tokP["end", a, g] for a in range(2) for g in range(2)]
            Scur, Snxt = S0, S1
            kS = [None, None]
            for g in range(2):
                kS[g] = setm(S0[:, 4 * g:4 * g + 4, :], 0.0, ends)
            st = {}
            for c in range(4):
                a, o = c // 2, 64 * (c % 2)
                rows_ = slice(o, o + 64)
                cols_ = slice(a * P + o, a * P + o + 64)
                for g in range(2):
                    hs = range(4 * g, 4 * g + 4)
                    hsl = slice(4 * g, 4 * g + 4)
                    bP, bQ = 3 + g, 5 + g
                    for j, h in enumerate(hs):
                        t = mm(PS[bP][rows_, j * P:(j + 1) * P], gk[:, h, cols_], Scur[:, h, :], True, True, kS[g],
                               tokP["c", a, g], bank_free[bP], sig=j == 3, loose=True)
                    for j, h in enumerate(hs):
                        mm(PS[bQ][rows_, j * P:(j + 1) * P], qd[:, h, cols_], Scur[:, h, :], j == 0, False, bank_free[bQ],
                           loose=True)
                    kv = tt(dve, VN[rows_, hsl, :], gv[rows_, hsl, a * P:(a + 1) * P],
                            PS[bP][rows_, :].rearrange("p (h d) -> p h d", h=4), ALU.subtract, t, tokP["v", a, g],
                            st.get(("vn", g)), ends)
                    bank_free[bP] = [kv]
                    if c < 3:
                        st["sd", g] = tt(pool, Sd[:, hsl, :], Scur[:, hsl, :], last(DEC[:, c, hsl], P), ALU.mult, kS[g],
                                         st.get(("sn", g)), ends)
                    st["kv", g] = kv
                    yield
                yield
                for g in range(2):
                    hs = range(4 * g, 4 * g + 4)
                    hsl = slice(4 * g, 4 * g + 4)
                    bQ, bS = 5 + g, 3 + g
                    pe.wait([st["kv", g], tokP["att", a, g], tokP["kd", a, g]])
                    if c < 3:
                        for j, h in enumerate(hs):
                            t = mm(PS[bS][:, j * P:(j + 1) * P], kb[rows_, h, a * P:(a + 1) * P], VN[rows_, h, :], True, True,
                                   bank_free[bS], sig=j == 3, loose=True)
                        kS[g] = tt(dve, Snxt[:, hsl, :], Sd[:, hsl, :], PS[bS][:].rearrange("p (h d) -> p h d", h=4),
                                   ALU.add, t, st["sd", g], st.get(("r", g)))
                        st["sn", g] = kS[g]
                        bank_free[bS] = [kS[g]]
                    for j, h in enumerate(hs):
                        t = mm(PS[bQ][rows_, j * P:(j + 1) * P], gq[rows_, h, cols_], VN[rows_, h, :], False, j == 3,
                               sig=j == 3, loose=True)
                    st["vn", g] = t
                    st["r", g] = t
                    k = afn(oSv[rows_, a, hsl, :], PS[bQ][rows_, :].rearrange("p (h d) -> p h d", h=4), ACT.Copy, t, ends)
                    bank_free[bQ] = [k]
                    tokP["o", c, g] = k
                    yield
                Scur, Snxt = Snxt, Scur
                if c % 2:
                    side.append(o_norm(a))

        def o_norm(a):
            al = [tokP["o", c, g] for c in (2 * a, 2 * a + 1) for g in range(2)] + [pe.now()]
            sq = kb[:, :, a * P:(a + 1) * P]
            yield from pause(2)
            k = afn(sq, oSv[:, a, :, :], ACT.Square, al)
            yield from pause(2)
            os_, fa, s2 = G_os[:, a, :], G_fac[:, a, :], G_sq[:, a, :]
            k = dve.do(lambda e: e.tensor_reduce(os_, sq, AX, ALU.add), k)
            k2 = ts(dve, s2, s2, 1e-6, 128e-6, ALU.add, ALU.mult, tokP["sq", a, 0], tokP["sq", a, 1])
            k = stt(os_, os_, 1.0 / 128, s2, ALU.mult, ALU.add, k, k2)
            k = tt(pool, fa, os_, npow[:, 0:8], ALU.pow, k)
            yield from pause(4)
            tokP["sc", a] = tt(dve, oSv[:, a, :, :], oSv[:, a, :, :], last(fa, P), ALU.mult, k)
            if a == 1:
                side.append(o_turn())

        def o_turn():
            sc = [tokP["sc", a] for a in range(2)]
            st = {}
            tmps = VN[:].rearrange("p h d -> p (h d)")
            while "xt2" not in tk:
                yield
            for i in range(4):
                b = 3 + i
                for j in range(2):
                    for a in range(2):
                        h = 2 * i + j
                        t = tr(PS[b][:, j * 256 + a * P:j * 256 + (a + 1) * P], oSv[:, a, h, :], sc, bank_free[b],
                               sig=j == 1 and a == 1)
                st[i] = t
            for i in range(4):
                b = 3 + i
                tmp = tmps[:, (i % 2) * 512:(i % 2) * 512 + 512]
                zz = gz[:, 2 * i:2 * i + 2, :].rearrange("p c t -> p (c t)")
                k = stt(tmp, PS[b][:], COLS[:, CG["gn"]:CG["gn"] + 1], zz, ALU.mult, ALU.mult, st[i], tk["gz", i],
                        st.get(("oa", i - 2)))
                bank_free[b] = [k]
                s = split(XH[:, 2 * i:2 * i + 2, :].rearrange("p c t -> p (c t)"),
                          XL[:, 2 * i:2 * i + 2, :].rearrange("p c t -> p (c t)"), tmp, [k], [tk["xt2"]])
                st["oa", i] = s
                tk["oa", 2 * i] = tk["oa", 2 * i + 1] = s
                yield

        def ob_of(q):
            return tk.get(("ob", q))

        def yb_evac(i):
            def evac(ps, t):
                k = tt(dve, mbv[:, 2 * i:2 * i + 2, :].rearrange("p c t -> p (c t)"), ps[:],
                       sgb[i % 2][:].rearrange("p c t -> p (c t)"), ALU.mult, t, tk["gb", i], tk["mbf"])
                tk["free", "gb", i + 2] = k
                tk["mb", i] = k
                return [k]
            return evac

        def fox_end():
            while "fox" not in tk:
                tick()
            for i in range(2):
                tk["free", "gb", i] = fence()
            tk["mbf"] = fence()

        for i in range(4):
            unit(w_cols(w2, 0, 8, GTB + 256 * i), 8, "B", XH, XL, xt_of, gate_evac(sgb[i % 2][:], "gb", i),
                 before=fox_end if i == 0 else None)
            unit(w_cols(w_proj_fox_2[0], 0, 8, 256 * i), 8, "B", obH, obL, ob_of, yb_evac(i))

        def ob_done():
            for i in range(4):
                tk["free", "gz", i] = tk["free", "ga2", i] = pe.now()

        for i in range(4):
            unit(w_cols(w2, 0, 8, GZ + 256 * i), 8, "B", XH, XL, xt_of,
                 gate_evac(gz[:, 2 * i:2 * i + 2, :], "gz", i, ACT.Silu), before=ob_done if i == 0 else None)
        for i in range(4):
            unit(w_cols(w2, 0, 8, GTA + 256 * i), 8, "B", XH, XL, xt_of, gate_evac(sg2[:, 2 * i:2 * i + 2, :], "ga2", i))

        def oa_of(q):
            return tk.get(("oa", q))

        m2_tok = [None] * 8

        def end_gdn():
            tk["xt2"] = pe.now()
            drain()
            tk["gdn_end"] = fence()

        def ya_evac(i):
            def evac(ps, t):
                sl = slice(2 * i, 2 * i + 2)
                v = sg2[:, sl, :]
                k = tt(dve, v.rearrange("p c t -> p (c t)"), ps[:], v.rearrange("p c t -> p (c t)"), ALU.mult, t,
                       tk["ga2", i])
                k2 = tt(pool, v, v, mbv[:, sl, :], ALU.add, k, tk["mb", i])
                m2_tok[2 * i] = m2_tok[2 * i + 1] = split(mH[:, sl, :], mL[:, sl, :], v, [k2], tk["gdn_end"])
                tk["m2"] = m2_tok[2 * i]
                return [k]
            return evac

        for i in range(4):
            unit(w_cols(w_proj_gdn_2[0], 0, 8, 256 * i), 8, "B", XH, XL, oa_of, ya_evac(i),
                 before=end_gdn if i == 0 else None)

        def m2_of(q):
            return m2_tok[q]

        res = {}

        def wo2_evac(i):
            def evac(ps, t):
                v = XRES[:, :, 256 * i:256 * i + 256]
                k = tt(dve, v, v, ps[:].rearrange("p (a n) -> p a n", a=2), ALU.add, t)
                res[i] = k
                return [k]
            return evac

        for i in range(4):
            unit(w_cols(w_out_2[0], 0, 8, 256 * i), 8, "A", mH, mL, m2_of, wo2_evac(i))

        f2H = reg("f2H", [P, FC2, T], 0, F32R)
        f2L = reg("f2L", [P, FC2, T], 32, F32R)
        rr = [reg(f"rr{i}", [P, 2, T], 64 + 2 * i) for i in range(3)]
        f2_tok = [None] * FC2

        def fourth_norm():
            xt_read["t"] = [pe.now()]
            xs_free["t"] = [tk["m2"], pool.now()]
            xr = [res[i] for i in range(4)]
            norm_to_xt(CG["mlp2"], [xr, xr])
            tk["f2"] = fence()

        def up2_evac(i):
            def evac(ps, t):
                r = rr[i % 3]
                k = afn(r[:].rearrange("p c t -> p (c t)"), ps[:], ACT.Relu, t, tk.get(("rr", i - 3)), tk["f2"])
                k2 = afn(f2H[:, 2 * i:2 * i + 2, :], r[:], ACT.Square, k, tk["f2"])
                k3 = tt(pool, r[:], r[:], r[:], ALU.mult, k2)

                def rest():
                    l = tt(dve, f2L[:, 2 * i:2 * i + 2, :], r[:], f2H[:, 2 * i:2 * i + 2, :].bitcast(F32), ALU.subtract,
                           k2, k3, tk["f2"])
                    tk["rr", i] = l
                    f2_tok[2 * i] = f2_tok[2 * i + 1] = [k2, l]
                defer(4, rest)
                return [k]
            return evac

        for i in range(FC2 // 2):
            unit(w_cols(w_up_2[0], 0, 8, 256 * i), 8, "B", XH, XL, xt_of, up2_evac(i),
                 before=fourth_norm if i == 0 else None)

        def f2_of(q):
            return f2_tok[q]

        outs = []
        ov = out[0].rearrange("(a p) n -> p a n", p=P)
        s_out = sem("s_out")

        def fin_evac(i):
            def evac(ps, t):
                v = XRES[:, :, 256 * i:256 * i + 256]
                k = tt(dve, v, v, ps[:].rearrange("p (a n) -> p a n", a=2), ALU.add, t)
                outs.append((i, k))
                return [k]
            return evac

        for i in range(4):
            for n in range(4):
                unit(w_cols(w_down_2[0], n * 8 * P, 8, 256 * i), 8, "A", f2H, f2L, f2_of, fin_evac(i), k0=8 * n,
                     first=n == 0, last_=n == 3)

        run_units()
        for i, k in outs:
            sp.wait([k])
            sp.prog.append(lambda e, i=i: e.dma_start(ov[:, :, 256 * i:256 * i + 256],
                                                      XRES[:, :, 256 * i:256 * i + 256]).then_inc(s_out, 16))
        sp.prog.append(lambda e: e.wait_ge(s_out, 64))

        block = ctx.enter_context(nc.Block())
        for q, name in ((sp, "sync"), (act, "scalar"), (dve, "vector"), (pool, "gpsimd"), (pe, "tensor")):
            def body(e, q=q):
                q.play(e)
            {"sync": block.sync, "scalar": block.scalar, "vector": block.vector, "gpsimd": block.gpsimd,
             "tensor": block.tensor}[name](body)


_INS = ["x", "norm_mix_pre", "w_in", "conv_mix_w", "w_att_branch", "w_conv_branch", "w_out", "norm_mix_post",
        "norm_ffn_pre", "w_up", "conv_ffn_w", "w_down", "norm_ffn_post", "norm_mix_g_2", "w_in_2", "gdn_conv_w_2",
        "gdn_a_log_2", "gdn_dt_bias_2", "gdn_norm_g_2", "fox_q_norm_g_2", "fox_k_norm_g_2", "fox_f_bias_2",
        "w_proj_gdn_2", "w_proj_fox_2", "w_out_2", "norm_mlp_g_2", "w_up_2", "w_down_2"]


def kernel(**inputs):
    import numpy as _np
    import concourse.bacc as _bacc
    from concourse.bass_utils import run_bass_kernel_spmd as _run

    nc = _bacc.Bacc("TRN2", target_bir_lowering=False, num_devices=1)
    arrays, args = {}, []
    for name in _INS:
        a = _np.ascontiguousarray(inputs[name])
        arrays[f"in_{name}"] = a
        args.append(nc.dram_tensor(f"in_{name}", a.shape, mybir.dt.from_np(a.dtype), kind="ExternalInput").ap())
    args.append(nc.dram_tensor("out_0", (1, T, D), F32, kind="ExternalOutput").ap())
    two_blocks(nc, *args)
    r = _run(nc, [arrays], core_ids=[0])
    return r.results[0]["out_0"]
```

```python
from contextlib import ExitStack

import concourse.bass as bass
from concourse import mybir

F32 = mybir.dt.float32
F32R = mybir.dt.float32r
ALU = mybir.AluOpType
ACT = mybir.ActivationFunctionType
AX = mybir.AxisListType.X

P = 128
T = 256
D = 1024
DC = D // P
NH = 8
DFF1 = 2816
FC1 = DFF1 // P
DFF2 = 4096
FC2 = DFF2 // P
NEG = -1e30
KB = 1024
NRAW = 3
NW = 3
AHEAD = 2
MAIN = 3
WARM = (12, 4, 12)
LO_A, HI_B, LO_B = 2, 2, 3
LATE_LO = [33, 67]
POOL_HALF = [*range(26, 33), *range(74, 98)]


class Queue:

    def __init__(self, sem, in_turn=False):
        self.sem, self.n, self.seen, self.prog, self.in_turn = sem, 0, {}, [], in_turn

    def wait(self, toks):
        for t in toks:
            if not t:
                continue
            if isinstance(t, list) or not isinstance(t[1], int):
                self.wait(t)
                continue
            sem, v = t
            if self.seen.get(sem.name, 0) < v:
                self.seen[sem.name] = v
                self.prog.append(lambda e, s=sem, v=v: e.wait_ge(s, v))

    def do(self, fn, *toks, sig=True):
        self.wait(toks)
        if self.in_turn and self.n:
            self.wait([self.now()])
        if not sig:
            self.prog.append(fn)
            return None
        self.n += 1
        self.prog.append(lambda e, s=self.sem: fn(e).then_inc(s, 1))
        return (self.sem, self.n)

    def now(self):
        return (self.sem, self.n)

    def play(self, e):
        for f in self.prog:
            f(e)


def two_blocks(nc, x, norm_mix_pre, w_in, conv_mix_w, w_att_branch, w_conv_branch, w_out, norm_mix_post,
               norm_ffn_pre, w_up, conv_ffn_w, w_down, norm_ffn_post, norm_mix_g_2, w_in_2, gdn_conv_w_2,
               gdn_a_log_2, gdn_dt_bias_2, gdn_norm_g_2, fox_q_norm_g_2, fox_k_norm_g_2, fox_f_bias_2,
               w_proj_gdn_2, w_proj_fox_2, w_out_2, norm_mlp_g_2, w_up_2, w_down_2, out):
    ctx = ExitStack()
    with ctx:
        base = 16640
        off = {"p": 0}

        def at(name, shape, o, dt=F32):
            return nc.alloc_sbuf_tensor_at(name, list(shape), dt, offset=base + int(o))

        def fixed(name, shape, dt=F32):
            n = 4
            for s in shape[1:]:
                n *= s
            t = at(name, shape, off["p"], dt)
            off["p"] += (n + 31) // 32 * 32
            return t

        def sem(name):
            return ctx.enter_context(nc.semaphore(name))

        RAW = [fixed(f"raw{i}", [P, 8, 256]) for i in range(NRAW)]
        WH = [fixed(f"wh{i}", [P, 8, 256], F32R) for i in range(NW)]
        WL = [fixed(f"wl{i}", [P, 8, 256], F32R) for i in range(NW)]
        XH = fixed("xh", [P, 8, T], F32R)
        XL = fixed("xl", [P, 8, T], F32R)
        XRES = fixed("xres", [P, 2, D])
        XS = fixed("xs", [P, 2, D])
        FG = fixed("fg", [P, 2, D])
        GP = fixed("gp", [P, D])
        ident = fixed("ident", [P, P])
        ones = fixed("ones", [P, P])
        TRI = fixed("tri", [P, P])
        UF = fixed("uf", [P, P])
        UI = fixed("ui", [P, P])
        UL = fixed("ul", [P, P])
        ONEB = fixed("oneb", [P, 2, P])
        MK3 = fixed("mk3", [P, 384])
        ML = fixed("ml", [P, 5, P])
        M1T = fixed("m1t", [P, P])
        COLS = fixed("cols", [P, 276])
        ss = fixed("ss", [P, 4])
        rs = fixed("rs", [P, 4])
        npow = fixed("npow", [P, 16])
        ppow = fixed("ppow", [P, 4])
        hb = fixed("hb", [P, 3, 8])
        gsm = fixed("gsm", [P, 2, 24])
        gv_ = fixed("gv_", [P, 12, 2, 8])
        DEC = fixed("dec", [P, 4, 8])
        CG = {"mix": 0, "ffn": 8, "mix2": 16, "mlp2": 24, "cmix": 32, "gn": 44, "fq": 45, "fk": 46,
              "cfa": 47, "cfg": 113, "gdn": 179}
        R0 = off["p"]
        assert base + R0 + 80 * KB <= nc.sbuf_usable_end, (base + R0 + 80 * KB, nc.sbuf_usable_end)

        def reg(name, shape, kb, dt=F32):
            return at(name, shape, R0 + kb * KB, dt)

        PS = [ctx.enter_context(nc.psum_tensor(f"ps{i}", [P, 512], F32)) for i in range(8)]

        pe, act, dve, pool, sp = (Queue(sem(f"s_{n}"), n == "pool") for n in ("pe", "act", "dve", "pool", "sp"))
        engines = (pe, act, dve, pool)

        later, side = [], []

        def defer(n, fn):
            later.append([n, fn])

        def run_later():
            while True:
                d = next((d for d in later if d[0] <= 0), None)
                if d is None:
                    return
                later.remove(d)
                d[1]()

        def flush():
            while later:
                m = min(d[0] for d in later)
                for d in later:
                    d[0] -= m
                run_later()

        def tick():
            for d in later:
                d[0] -= 1
            run_later()
            for g in list(side):
                if g in side and next(g, "end") == "end":
                    side.remove(g)

        def pause(n):
            for _ in range(n):
                yield

        def drain():
            while side:
                tick()
            flush()

        def fence():
            flush()
            return [q.now() for q in engines]

        def mm(o, l, r, start, stop, *toks, sig=False, loose=False):
            return pe.do(lambda e: e.matmul(o, l, r, start=start, stop=stop, skip_group_check=loose), *toks, sig=sig)

        def tr(o, i, *toks, sig=False):
            return pe.do(lambda e: e.transpose(o, i, ident[:]), *toks, sig=sig)

        def afn(o, i, f, *toks, **kw):
            return act.do(lambda e: e.activation(o, i, f, **kw), *toks)

        def tt(q, o, a, b, op, *toks):
            return q.do(lambda e: e.tensor_tensor(o, a, b, op), *toks)

        def ts(q, o, a, s1, s2, op0, op1, *toks):
            if op1 is None:
                return q.do(lambda e: e.tensor_scalar(o, a, s1, None, op0), *toks)
            return q.do(lambda e: e.tensor_scalar(o, a, s1, s2, op0, op1), *toks)

        def stt(o, a, s, b, op0, op1, *toks):
            return dve.do(lambda e: e.scalar_tensor_tensor(o, a, s, b, op0, op1), *toks)

        def mid(ap, n):
            return ap.unsqueeze(1).broadcast_to([ap.shape[0], n, ap.shape[1]])

        def last(ap, n):
            return ap.unsqueeze(2).broadcast_to([ap.shape[0], ap.shape[1], n])

        n_dma = [0]

        def load(q, dst, src):
            s = sem(f"ld{n_dma[0]}")
            n_dma[0] += 1
            q.prog.append(lambda e: e.dma_start(dst, src).then_inc(s, 16))
            return (s, 16)

        xv = x[0].rearrange("(a p) n -> p a n", p=P)
        x_in = [load(sp, XRES[:, a, :], xv[:, a, :]) for a in range(2)]
        R1 = reg("r1", [P, P], 76)
        R2 = reg("r2", [P, P], 76.5)
        R3 = reg("r3", [P, P], 77)
        R4 = reg("r4", [P, P], 77.5)
        rows = []

        def row(dst, src, q=sp):
            rows.append(load(q, dst, src))

        chunks = "a (c p) -> (a c) p"
        row(R1[0:8, :], norm_mix_pre.rearrange(chunks, p=P), act)
        hb_in = []

        def late_rows():
            row(R1[8:16, :], norm_ffn_pre.rearrange(chunks, p=P))
            row(R1[16:24, :], norm_mix_g_2.rearrange(chunks, p=P))
            row(R1[24:32, :], norm_mlp_g_2.rearrange(chunks, p=P))
            row(R1[32:44, :], conv_mix_w[0].rearrange(chunks, p=P))
            row(R1[44:45, :], gdn_norm_g_2)
            row(R1[45:46, :], fox_q_norm_g_2)
            row(R1[46:47, :], fox_k_norm_g_2)
            for k in range(3):
                row(R2[22 * k:22 * k + 22, :], conv_ffn_w[0, k:k + 1, 0:DFF1].rearrange(chunks, p=P))
                row(R3[22 * k:22 * k + 22, :], conv_ffn_w[0, k:k + 1, DFF1:2 * DFF1].rearrange(chunks, p=P))
            row(R4[0:96, :], gdn_conv_w_2[0].rearrange(chunks, p=P))
            hb_in.extend([load(sp, hb[:, i, :], v[0].partition_broadcast(P))
                     for i, v in enumerate((gdn_dt_bias_2, gdn_a_log_2, fox_f_bias_2))])

        def setm(ap, v, *toks):
            return pool.do(lambda e: e.memset(ap, v), *toks)

        def sel(ap, cmp, fill, base_, pattern, cm, *toks):
            return pool.do(lambda e: e.affine_select(out=ap, in_=ap, compare_op=cmp, fill=fill, base=base_,
                                                     pattern=pattern, channel_multiplier=cm), *toks)

        k = setm(ident[:], 0.0)
        c_id = sel(ident[:], ALU.not_equal, 1.0, 0, [[-1, P]], 1, k)
        c_np = setm(npow[:], -0.5)
        c_on = setm(ones[:], 1.0)
        k = setm(TRI[:], 1.0)
        c_tri = sel(TRI[:], ALU.is_ge, 0.0, 0, [[-1, P]], 1, k)
        late = []

        def late_constants():
            k = setm(UF[:], 1.0)
            late.append(sel(UF[:], ALU.is_ge, 0.0, 0, [[1, P]], -1, k))
            for m, cmp, b_, st, cm in ((UI, ALU.is_ge, 0, 1, -1), (UL, ALU.is_gt, 0, -1, 1)):
                k = setm(m[:], 1.0)
                k = sel(m[:], cmp, 0.0, b_, [[st, P]], cm, k)
                if cm < 0:
                    late.append(setm(m[0:64, 64:128], 0.0, k))
                else:
                    late.append(setm(m[64:128, 0:64], 0.0, k))
            k = setm(ONEB[:], 0.0)
            late.append(setm(ONEB[0:64, 0, :], 1.0, k))
            late.append(setm(ONEB[64:128, 1, :], 1.0, k))
            k = setm(MK3[:], 0.0)
            for b in (0, 256):
                late.append(sel(MK3[:, b:b + 128], ALU.is_ge, NEG, 0, [[-1, P]], 1, k))
            k = setm(ML[:], 0.0)
            for i, b in enumerate((2, 4, 8, 16, 32)):
                nb = P // (2 * b)
                v = ML[:, i, :].rearrange("p (n z b) -> p n z b", z=2, b=b)[:, :, 0, :]
                k2 = setm(v, -1.0, k)
                k2 = sel(v, ALU.is_ge, 0.0, -b, [[-2 * b, nb], [0, b]], 1, k2)
                late.append(sel(v, ALU.is_ge, 0.0, 2 * b - 1, [[2 * b, nb], [0, b]], -1, k2))
            k = setm(M1T[:], 0.0)
            v = M1T[:].rearrange("p (n z) -> p n z", z=2)[:, :, 1]
            late.append(sel(v, ALU.not_equal, -1.0, 0, [[-2, 64]], 1, k))
            late.append(setm(ppow[:], 0.5))

        raw_sem = [sem(f"rw{i}") for i in range(NRAW)]
        raw_cnt = [0] * NRAW
        raw_free = [[] for _ in range(NRAW)]
        w_free = [[] for _ in range(NW)]
        bank_free = {i: [] for i in range(8)}
        units = []
        state = {"prep": 0, "bank": 0}

        def do_load(i):
            u = units[i]
            s = i % NRAW
            sp.wait(raw_free[s])
            raw_cnt[s] += 16
            dst, src = RAW[s][:, 0:u["kc"], :], u["src"]
            sp.prog.append(lambda e: e.dma_start(dst, src).then_inc(raw_sem[s], 16))
            u["raw"] = (raw_sem[s], raw_cnt[s])

        def do_prep(i):
            u = units[i]
            s, w, kc = i % NRAW, i % NW, u["kc"]
            u["ready"] = []
            half = (kc + 1) // 2

            def hi(a, b):
                return afn(WH[w][:, a:b, :], RAW[s][:, a:b, :], ACT.Copy, u["raw"], w_free[w])

            def lo(q, a, b, h):
                k = tt(q, WL[w][:, a:b, :], RAW[s][:, a:b, :], WH[w][:, a:b, :].bitcast(F32), ALU.subtract, h, w_free[w])
                u["ready"] += [(h, k)] * (b - a)

            def second():
                h = hi(half, kc)

                def end():
                    lo(pool if i in POOL_HALF else dve, half, kc, h)
                    raw_free[s] = [u["ready"][0], u["ready"][-1]]
                    if i + NRAW < len(units):
                        do_load(i + NRAW)
                defer(20 if i in LATE_LO else LO_B, end)
            h = hi(0, half)
            defer(LO_A, lambda: lo(dve, 0, half, h))
            defer(HI_B, second)
            if i == 0:
                flush()

        def prep_next(to):
            while state["prep"] <= to:
                do_prep(state["prep"])
                state["prep"] += 1

        def unit(src, kc, mode, xh, xl, xtok, evac, k0=0, first=True, last_=True, before=None, halves=False, fresh=False):
            units.append(dict(src=src, kc=kc, mode=mode, xh=xh, xl=xl, xtok=xtok, evac=evac, k0=k0, first=first,
                              last=last_, before=before, halves=halves,
                              fresh=fresh))

        def run_units():
            for i in range(NRAW):
                do_load(i)
            late_rows()
            for i, u in enumerate(units):
                if u["before"]:
                    u["before"]()
                prep_next(min(len(units) - 1, i + AHEAD))
                w, kc, k0 = i % NW, u["kc"], u["k0"]
                bk = state["bank"] % MAIN
                whole = u["first"] and u["last"]
                tok = None
                for c in range(2):
                    hb_ = MAIN + bk if u["halves"] and c else bk
                    if u["first"] and (c == 0 or u["halves"]):
                        pe.wait(bank_free[hb_])
                    o = PS[hb_][:, 0:256] if u["halves"] else PS[bk][:, c * 256:(c + 1) * 256]
                    order = [(q, j) for q in range(kc) for j in range(3)]
                    if u["fresh"] and c == 0:
                        order = [(q, j) for q in range(kc) for j in (0, 2)] + [(q, 1) for q in range(kc)]
                    for n, (q, j) in enumerate(order):
                        while len(u["ready"]) <= q or u["xtok"](k0 + q) is None:
                            tick()
                        xt = u["xtok"](k0 + q)
                        if u["fresh"] and j != 1:
                            xt = xt[0]
                        pe.wait([u["ready"][q], xt])
                        xh, xl = u["xh"][:, k0 + q, :], u["xl"][:, k0 + q, :]
                        wh, wl = WH[w][:, q, :], WL[w][:, q, :]
                        cs = slice(c * P, (c + 1) * P)
                        if u["mode"] == "B":
                            l, r = ((wh, xh), (wh, xl), (wl, xh))[j]
                            l = l[:, cs]
                        else:
                            l, r = ((xh, wh), (xl, wh), (xh, wl))[j]
                            l = l[:, cs]
                        st = n == 0 and (u["first"] and (whole or c == 0 or u["halves"]))
                        end = n == 3 * kc - 1
                        tok = mm(o, l, r, st, end and u["last"], sig=end, loose=not whole)
                        if n % 6 == 5:
                            tick()
                    if u["halves"] and u["last"]:
                        bank_free[hb_] = u["evac"](o, tok, c)
                w_free[w] = [tok]
                if u["last"]:
                    if not u["halves"]:
                        bank_free[bk] = u["evac"](PS[bk], tok)
                    state["bank"] += 1

        xt_tok = [None] * 8
        xt_read = {"t": []}

        sc = [None, None]

        def squares(a, xtok):
            return afn(XS[:, a, :], XRES[:, a, :], ACT.Square, xtok, xs_free["t"], accum_out=ss[:, a:a + 1])

        def rstd(a, c, k):
            k = ts(pool, rs[:, a:a + 1], ss[:, c:c + 1], 1.0 / D, 1e-6, ALU.mult, ALU.add, k)
            return tt(pool, rs[:, 2 + a:3 + a], rs[:, a:a + 1], npow[:, 0:1], ALU.pow, k, c_np)

        def scaled(a, k, sq):
            sc[a] = [ts(dve, XS[:, a, u:u + 512], XRES[:, a, u:u + 512], rs[:, 2 + a:3 + a], None, ALU.mult, None, k, sq)
                     for u in (0, 512)]

        def norm_scale(x0, x1):
            q0, q1 = squares(0, x0), squares(1, x1)
            scaled(0, rstd(0, 0, q0), q0)
            scaled(1, rstd(1, 1, q1), q1)

        def exp_ln_table():
            act.prog.append(lambda e: e.preload_act_table_set("natural_log_exp_and_others"))

        def keep_warm(n):
            pe.wait([c_id, bank_free[7]])
            for _ in range(n):
                mm(PS[7][:, 0:P], ident[:], ident[:], True, True)

        def norm_to_xt(gcol, gtok=(), between=None):
            free = xt_read["t"]
            turned = {}
            for a in range(2):
                if a and not between:
                    keep_warm(WARM[1])
                for c in range(8):
                    b, j = 3 + c // 2, c % 2
                    t = tr(PS[b][:, j * 256 + a * P:j * 256 + (a + 1) * P], XS[:, a, c * P:(c + 1) * P],
                           sc[a][c // 4], c_id, bank_free[b], sig=a == 1)
                    turned[c] = t
            for g in range(4):
                if g == 2 and between:
                    between()
                b = 3 + g
                hs = [afn(XH[:, c, :], PS[b][:, (c % 2) * 256:(c % 2 + 1) * 256], ACT.Identity, turned[2 * g + 1], free, gtok,
                          scale=COLS[:, gcol + c:gcol + c + 1]) for c in (2 * g, 2 * g + 1)]
                for c in (2 * g, 2 * g + 1):
                    lo = stt(XL[:, c, :], PS[b][:, (c % 2) * 256:(c % 2 + 1) * 256], COLS[:, gcol + c:gcol + c + 1],
                             XH[:, c, :].bitcast(F32), ALU.mult, ALU.subtract, hs, free)
                    xt_tok[c] = [hs[c % 2], lo]
                bank_free[b] = [lo]
            xs_free["t"] = [t]

        xs_free = {"t": []}

        def split(hi, lo, src, toks, free=(), q=None):
            h = afn(hi, src, ACT.Copy, list(toks), list(free))
            l = tt(q or dve, lo, src, hi.bitcast(F32), ALU.subtract, h, list(free))
            return [h, l]

        def split_later(hi, lo, src, toks, free, got, now=False):
            if now:
                got(split(hi, lo, src, toks, free))
                return

            def first():
                h = afn(hi, src, ACT.Copy, list(toks), list(free))
                defer(2, lambda: got([h, tt(dve, lo, src, hi.bitcast(F32), ALU.subtract, h, list(free))]))
            defer(1, first)

        def w_cols(w, r0, kc, c0, n=256):
            return w[r0:r0 + kc * P, c0:c0 + n].rearrange("(k p) n -> p k n", p=P)

        def xt_of(q):
            return xt_tok[q]

        qT = reg("qT", [P, 4, T], 0)
        kT = reg("kT", [P, 4, T], 4)
        vS = reg("vS", [P, 2, 512], 8)
        ccs = [reg(f"ccs{i}", [P, 2, T], 12 + 2 * i) for i in range(2)]
        pp = reg("pp", [P, 2, T], 16)
        cvy = reg("cvy", [P, 2, T], 18)
        att = [[reg(f"at{n}{i}", [P, 384], 25 + 1.5 * (2 * n + i)) for i in range(2)] for n in range(4)]
        ycH = reg("ycH", [P, 4, T], 37, F32R)
        ycL = reg("ycL", [P, 4, T], 41, F32R)
        oH = reg("oH", [P, 4, T], 45, F32R)
        oL = reg("oL", [P, 4, T], 49, F32R)
        sga = reg("sga", [P, 8, T], 53)
        sgc = [reg(f"sgc{i}", [P, 2, T], 61 + 2 * i) for i in range(2)]
        mcv = reg("mcv", [P, 8, T], 65)
        mt = [reg(f"mt{i}", [P, 2, T], 73 + 2 * i) for i in range(2)]

        def gains():
            t = pe.do(lambda e: e.transpose(PS[7][:, 0:8], R1[0:8, :], ident[0:8, 0:8]), rows[0], c_id)
            k = dve.do(lambda e: e.tensor_copy(COLS[:, 0:8], PS[7][:, 0:8]), t)
            bank_free[7] = [k]
            return k

        def head_rows():
            yield from pause(12)
            late_constants()
            yield from pause(4)
            t = bank_free[7]
            for src, n, c in ((R1, 47, 0), (R2, 66, 47), (R3, 66, 113), (R4, 96, 179)):
                t = pe.do(lambda e, src=src, n=n, c=c: e.transpose(PS[7][:, c:c + n], src[0:n, :], ident[0:n, 0:n]),
                          rows, t)
            yield
            t = dve.do(lambda e: e.tensor_copy(COLS[:, 8:275], PS[7][:, 8:275]), t)
            bank_free[7] = [t]
            tk["cols"] = t

        tk = {}
        exp_ln_table()

        def first_norm():
            keep_warm(WARM[2])
            g = gains()
            norm_scale(*x_in)
            norm_to_xt(CG["mix"], g, lambda: prep_next(0))
            side.append(head_rows())


        w = w_in[0]
        A0, A1, A2 = 0, 512, 1024
        C0, C1, C2 = 1536, 2048, 2560
        GA, GC = 3072, 4096

        def keep(dst, key, i, scale=1.0):
            def evac(ps, t):
                k = act.do(lambda e: e.activation(dst[:, 2 * i:2 * i + 2, :].rearrange("p c t -> p (c t)"), ps[:],
                                                  ACT.Copy, scale=scale), t)
                tk[key, i] = k
                return [k]
            return evac

        for i in range(2):
            unit(w_cols(w, 0, 8, A0 + 256 * i), 8, "B", XH, XL, xt_of, keep(qT, "q", i, 0.125),
                 before=first_norm if i == 0 else None, fresh=i == 0)
        for i in range(2):
            unit(w_cols(w, 0, 8, A1 + 256 * i), 8, "B", XH, XL, xt_of, keep(kT, "k", i))
        for i in range(2):
            def v_evac(ps, t, i=i):
                k = afn(vS[:, :, 256 * i:256 * i + 256], ps[:].rearrange("p (a n) -> p a n", a=2), ACT.Copy, t)
                tk["v", i] = k
                return [k]
            unit(w_cols(w, 0, 8, A2 + 256 * i), 8, "A", XH, XL, xt_of, v_evac)

        def cc_evac(ps, t):
            k = afn(ccs[0][:].rearrange("p c t -> p (c t)"), ps[:], ACT.Copy, t, tk.get("pp"))
            tk["cc"] = k
            return [k]

        def cx_evac(i):
            def evac(ps, t):
                c0 = CG["cmix"]
                k = tt(dve, pp[:].rearrange("p c t -> p (c t)"), ps[:], ccs[0][:].rearrange("p c t -> p (c t)"),
                       ALU.mult, t, tk["cc"], tk.get("cvy"))
                tk["pp"] = k

                def wc(j, n):
                    c = c0 + 4 * n + 2 * i + j
                    return COLS[:, c:c + 1]
                ys = [afn(cvy[:, j, :], pp[:, j, :], ACT.Identity, k, tk.get("yc"), tk["cols"], scale=wc(j, 2))
                      for j in range(2)]

                def rest():
                    tk["cvy"] = []
                    for j in range(2):
                        y = stt(cvy[:, j, 1:T], pp[:, j, 0:T - 1], wc(j, 1), cvy[:, j, 1:T], ALU.mult, ALU.add, ys[j])
                        y = stt(cvy[:, j, 2:T], pp[:, j, 0:T - 2], wc(j, 0), cvy[:, j, 2:T], ALU.mult, ALU.add, y)
                        tk["cvy"].append(y)
                    tk["pp"] = y
                defer(2, rest)
                return [k]
            return evac

        def cb_evac(i):
            def evac(ps, t):
                k = tt(dve, cvy[:].rearrange("p c t -> p (c t)"), ps[:], cvy[:].rearrange("p c t -> p (c t)"), ALU.mult,
                       t, tk["cvy"])

                def got(s):
                    tk["yc"] = s
                    tk["ycT", 2 * i] = tk["ycT", 2 * i + 1] = s
                split_later(ycH[:, 2 * i:2 * i + 2, :], ycL[:, 2 * i:2 * i + 2, :], cvy[:], [k], (), got)
                return [k]
            return evac

        def attention(e_):
            zs, e, s_, d = (att[n][e_] for n in range(4))
            bz, bc = 3 + 2 * e_, 4 + 2 * e_
            z, C, O = PS[bz], PS[bc], PS[7]
            o_free = bank_free[7]

            def diag(ap):
                return ap[:].rearrange("p (b t) -> p b t", b=3)[:, 0::2, :]

            k_o = None
            for h in range(e_, NH, 2):
                c, o = h // 2, 64 * e_
                kk, qq = kT[o:o + 64, c, :], qT[o:o + 64, c, :]
                while ("k", c // 2) not in tk:
                    yield
                mm(z[:, 0:256], kk[:, 0:P], qq, True, True, tk["q", c // 2], tk["k", c // 2], bank_free[bz])
                t = mm(z[:, 256:384], kk[:, P:T], qq[:, P:T], True, True, sig=True)
                yield
                z0 = afn(zs[:], z[:, 0:384], ACT.Copy, t)
                bank_free[bz] = [z0]
                a = afn(e[:], zs[:], ACT.Abs, z0)
                a = afn(e[:], e[:], ACT.Exp, a, scale=-1.0)
                a = afn(e[:], e[:], ACT.Ln, a, bias=1.0)
                yield from pause(5)
                k = stt(s_[:], zs[:], 0.0, e[:], ALU.max, ALU.add, a, z0)
                v = diag(s_)
                ks = pool.do(lambda en: en.affine_select(
                    out=v, in_=v, compare_op=ALU.is_gt, fill=0.0, base=0, pattern=[[0, 2], [1, P]],
                    channel_multiplier=-1), k)
                yield from pause(4)
                mm(C[:, 0:256], TRI[:], s_[:, 0:256], True, False, ks, c_tri, bank_free[bc], loose=True)
                mm(C[:, 128:256], ones[:], s_[:, 256:384], False, True, c_on, loose=True)
                t = mm(C[:, 256:384], TRI[:], s_[:, 256:384], True, True, sig=True, loose=True)
                yield
                k = tt(dve, d[:], zs[:], C[:, 0:384], ALU.subtract, t, z0, k_o)
                bank_free[bc] = [k]
                w_ = diag(d)
                k = pool.do(lambda en: en.affine_select(
                    out=w_, in_=w_, compare_op=ALU.is_gt, fill=NEG, base=0, pattern=[[0, 2], [1, P]],
                    channel_multiplier=-1), k)
                yield from pause(4)
                k = afn(d[:], d[:], ACT.Exp, k)
                yield from pause(2)
                while ("v", h // 4) not in tk:
                    yield
                mm(O[o:o + 64, 0:256], vS[:, 0, h * 64:(h + 1) * 64], d[:, 0:256], True, False, k, tk["v", h // 4],
                   o_free, loose=True)
                k_o = mm(O[o:o + 64, 128:256], vS[:, 1, h * 64:(h + 1) * 64], d[:, 256:384], False, True, sig=True,
                         loose=True)
                yield
                hh = afn(oH[o:o + 64, c, :], O[o:o + 64, 0:256], ACT.Copy, k_o)
                yield from pause(2)
                ll = tt(dve, oL[o:o + 64, c, :], O[o:o + 64, 0:256], oH[o:o + 64, c, :].bitcast(F32), ALU.subtract, hh)
                o_free = bank_free[7] = [hh, ll]
                tk["oT", h] = [hh, ll]

        def start_attention():
            side.extend(attention(e_) for e_ in range(2))

        for i in range(2):
            unit(w_cols(w, 0, 8, C1 + 256 * i), 8, "B", XH, XL, xt_of, cc_evac,
                 before=start_attention if i == 0 else None)
            unit(w_cols(w, 0, 8, C2 + 256 * i), 8, "B", XH, XL, xt_of, cx_evac(i))
            unit(w_cols(w, 0, 8, C0 + 256 * i), 8, "B", XH, XL, xt_of, cb_evac(i))

        def gate_evac(dst, key, i, f=ACT.Sigmoid):
            def evac(ps, t):
                k = afn(dst, ps[:].rearrange("p (c t) -> p c t", c=2), f, t, tk.get(("free", key, i)))
                tk[key, i] = k
                if key == "gc" and side:
                    exp_ln_table()
                return [k]
            return evac

        def yc_of(q):
            return tk.get(("ycT", q))

        def ycv_evac(i):
            def evac(ps, t):
                k = tt(dve, mcv[:, 2 * i:2 * i + 2, :].rearrange("p c t -> p (c t)"), ps[:],
                       sgc[i % 2][:].rearrange("p c t -> p (c t)"), ALU.mult, t, tk["gc", i])
                tk["free", "gc", i + 2] = k
                tk["mc", i] = k
                return [k]
            return evac

        for i in range(4):
            unit(w_cols(w, 0, 8, GC + 256 * i), 8, "B", XH, XL, xt_of, gate_evac(sgc[i % 2][:], "gc", i),
                 before=None)
            unit(w_cols(w_conv_branch[0], 0, 4, 256 * i), 4, "B", ycH, ycL, yc_of, ycv_evac(i))

        for i in range(4):
            unit(w_cols(w, 0, 8, GA + 256 * i), 8, "B", XH, XL, xt_of, gate_evac(sga[:, 2 * i:2 * i + 2, :], "ga", i))

        def o_of(q):
            if ("oT", 2 * q) in tk and ("oT", 2 * q + 1) in tk:
                return [tk["oT", 2 * q], tk["oT", 2 * q + 1]]
            return None

        m_tok = [None] * 8

        def yat_evac(i):
            def evac(ps, t):
                sl = slice(2 * i, 2 * i + 2)
                m = mt[i % 2]
                if i == 0:
                    xt_read["t"] = [tk["xt_done"]]
                k = tt(dve, m[:].rearrange("p c t -> p (c t)"), ps[:], sga[:, sl, :].rearrange("p c t -> p (c t)"),
                       ALU.mult, t, tk["ga", i], tk.get(("mt", i - 2)))
                k2 = tt(dve, m[:], m[:], mcv[:, sl, :], ALU.add, k, tk["mc", i])

                def got(s):
                    tk["mt", i] = s
                    m_tok[2 * i] = m_tok[2 * i + 1] = s
                split_later(XH[:, sl, :], XL[:, sl, :], m[:], [k2], xt_read["t"], got, i == 3)
                return [k]
            return evac

        def y_att_start():
            tk["xt_done"] = pe.now()
            drain()

        for i in range(4):
            unit(w_cols(w_att_branch[0], 0, 4, 256 * i), 4, "B", oH, oL, o_of, yat_evac(i),
                 before=y_att_start if i == 0 else None)

        def m_of(q):
            return m_tok[q]

        def post_evac(i, gtok):
            def evac(ps, t, a):
                k = afn(FG[:, a, 256 * i:256 * i + 256], ps, ACT.Square, t, tk.get("fg_free"),
                        accum_out=gv_[:, 11, a, i:i + 1])
                if i == 3:
                    sq = [tk["sq", a, n] for n in range(3)] + [k]
                    kr = dve.do(lambda e: e.tensor_reduce(ss[:, 2 + a:3 + a], gv_[:, 11, a, 0:4], AX, ALU.add), sq)
                g = tt(dve, FG[:, a, 256 * i:256 * i + 256], ps, GP[:, 256 * i:256 * i + 256], ALU.mult, k, tk[gtok])
                tk["sq", a, i], tk["po", a, i] = k, [k, g]
                if i == 3:
                    al = [tk["po", a, n] for n in range(4)]
                    q0 = squares(0, tk["x", 0]) if a else None
                    k = rstd(a, 2 + a, kr)
                    k0 = rstd(0, 0, [q0, tk["x", 0]]) if a else None
                    tk["x", a] = stt(XRES[:, a, :], FG[:, a, :], rs[:, 2 + a:3 + a], XRES[:, a, :], ALU.mult, ALU.add, k, al)
                    if a:
                        scaled(0, k0, q0)
                        q1 = squares(1, tk["x", 1])
                        k1 = rstd(1, 1, [q1, tk["x", 1]])
                        flush()
                        scaled(1, k1, q1)
                return [g]
            return evac

        tk["g_post"] = load(sp, GP[:], norm_mix_post[0].partition_broadcast(P))
        for i in range(4):
            unit(w_cols(w_out[0], 0, 8, 256 * i), 8, "A", XH, XL, m_of, post_evac(i, "g_post"),
                 halves=True, fresh=i == 0)

        fH = reg("fH", [P, FC1, T], 0, F32R)
        fL = reg("fL", [P, FC1, T], 22, F32R)
        ya = [reg(f"ya{i}", [P, 2, T], 44 + 2 * i) for i in range(2)]
        yg = [reg(f"yg{i}", [P, 2, T], 48 + 2 * i) for i in range(2)]
        f_tok = [None] * FC2
        gsw = reg("gsw", [P, 8, 24], 76)
        gswH = reg("gswH", [P, 8, 24], 76.75, F32R)
        gswL = reg("gswL", [P, 8, 24], 77.5, F32R)
        GSA, FFO = 4096, 7184

        def second_norm():
            xt_read["t"] = [pe.now()]
            tk["fg_free"] = [tk["x", 0], tk["x", 1]]
            sp.wait(fence())
            tk["g_post2"] = load(sp, GP[:], norm_ffn_post[0].partition_broadcast(P))
            ga = load(sp, gsw[:, :, 0:16], w_in_2[0][:, GSA:GSA + 16].rearrange("(k p) n -> p k n", p=P))
            gf = load(sp, gsw[:, :, 16:24], w_in_2[0][:, FFO:FFO + 8].rearrange("(k p) n -> p k n", p=P))
            keep_warm(WARM[0])
            norm_to_xt(CG["ffn"])
            f = tk["ffn_f"] = fence()

            def small_weights():
                tk["gsw"] = split(gswH[:], gswL[:], gsw[:], [ga, gf], f)
            defer(20, small_weights)

        def conv_evac(dst, cbase, nch, taps, c0, key, fin):
            def evac(ps, t):
                ys = []
                for j in range(2):
                    def wc(n, c=c0 + j):
                        return COLS[:, cbase + nch * n + c:cbase + nch * n + c + 1]
                    ys.append(afn(dst[:, j, :], ps[:, j * 256:(j + 1) * 256], ACT.Identity, t, tk.get(("free", key)),
                                  tk.get("ffn_f"), scale=wc(taps - 1)))
                done, free = [], []

                def rest(j):
                    def wc(n, c=c0 + j):
                        return COLS[:, cbase + nch * n + c:cbase + nch * n + c + 1]
                    y = ys
                    for d in range(1, taps):
                        y = stt(dst[:, j, d:T], ps[:, j * 256:j * 256 + T - d], wc(taps - 1 - d), dst[:, j, d:T], ALU.mult,
                                ALU.add, y)
                    done.append(y)
                    if j:
                        free.append(y)
                        fin(done)
                    else:
                        defer(2, lambda: rest(1))
                defer(1, lambda: rest(0))
                return free
            return evac

        for i in range(FC1 // 2):
            def fin_a(done, i=i):
                tk["ya", i] = done

            def fin_g(done, i=i):
                s = i % 2

                def got(r):
                    tk["free", "ya", i + 2] = r
                    f_tok[2 * i] = f_tok[2 * i + 1] = r

                def product():
                    k = afn(yg[s][:], yg[s][:], ACT.Gelu_apprx_tanh, done)
                    k = tt(pool, ya[s][:], ya[s][:], yg[s][:], ALU.mult, k, tk["ya", i])
                    tk["free", "yg", i + 2] = k
                    defer(3, lambda: split_later(fH[:, 2 * i:2 * i + 2, :], fL[:, 2 * i:2 * i + 2, :], ya[s][:], [k],
                                                 tk["ffn_f"], got))
                defer(2, product)

            unit(w_cols(w_up[0], 0, 8, 256 * i), 8, "B", XH, XL, xt_of,
                 (lambda ps, t, i=i, f=fin_a: conv_evac(ya[i % 2], CG["cfa"], FC1, 3, 2 * i, ("x", i), f)(ps, [t, tk.get(("free", "ya", i))])),
                 before=second_norm if i == 0 else None, fresh=i == 0)
            unit(w_cols(w_up[0], 0, 8, DFF1 + 256 * i), 8, "B", XH, XL, xt_of,
                 (lambda ps, t, i=i, f=fin_g: conv_evac(yg[i % 2], CG["cfg"], FC1, 3, 2 * i, ("x", i), f)(ps, [t, tk.get(("free", "yg", i))])))

        def f_of(q):
            return f_tok[q]

        for i in range(4):
            for n, (r0, kc) in enumerate(((0, 8), (8, 8), (16, 6))):
                unit(w_cols(w_down[0], r0 * P, kc, 256 * i), kc, "A", fH, fL, f_of, post_evac(i, "g_post2"), halves=True,
                     k0=r0, first=n == 0, last_=n == 2)

        gq = reg("gq", [P, 8, T], 0)
        gk = reg("gk", [P, 8, T], 8)
        gv = reg("gv", [P, 8, T], 16)
        fqm = reg("fqm", [P, 2, D], 24)
        fkm = reg("fkm", [P, 2, D], 32)
        fvm = reg("fvm", [P, 2, D], 40)
        fqT = XS[:].rearrange("p a (c t) -> p (a c) t", t=T)
        fkT = fqm[:].rearrange("p a (h d) -> p h a d", h=8)
        jk = [reg(f"jk{i}", [P, 512], 2 * i) for i in range(2)]
        sS = [reg(f"sS{i}", [P, 384], 48 + 1.5 * i) for i in range(2)]
        sT = [reg(f"sT{i}", [P, 384], 51 + 1.5 * i) for i in range(2)]
        CL = reg("CL", [64, T], 54)
        CX = reg("CX", [64, T], 55)
        CR = [reg(f"CR{i}", [64, T], 56 + i) for i in range(2)]
        stt2 = reg("stt2", [P, 8, 8], 58)
        HM = reg("HM", [64, 8], 58.5)
        gst = reg("gst", [24, T], 59)
        obH = reg("obH", [P, 8, T], 60, F32R)
        obL = reg("obL", [P, 8, T], 68, F32R)
        E = FG
        Ev = E[:].rearrange("p a (h t) -> p a h t", h=8)
        (G_g, G_beta, G_G, G_os, G_eG, G_lf, G_dec, G_sq, G_sk, G_D, G_Dd, G_rt) = (gv_[:, i, :, :] for i in range(12))
        G_gl, G_fac = G_os, G_lf

        w2 = w_in_2[0]
        GQ, GK, GV, GZ = 0, 1024, 2048, 3072
        FQ, FK, FV = 4112, 5136, 6160
        GTA, GTB = 7192, 8216

        def third_norm():
            xt_read["t"] = [pe.now()]
            tk["fg_free"] = [tk["x", 0], tk["x", 1]]
            keep_warm(WARM[0])
            norm_to_xt(CG["mix2"])
            tk["b2"] = fence()
            exp_ln_table()
            side.append(small_side())

        def softplus(dst, src, tmp, toks, sign=1.0):
            a = afn(tmp, src, ACT.Abs, toks)
            a = afn(tmp, tmp, ACT.Exp, a, scale=-1.0)
            a = afn(tmp, tmp, ACT.Ln, a, bias=1.0)
            m = ts(dve, dst, src, sign, 0.0, ALU.mult, ALU.max, a)
            return tt(dve, dst, dst, tmp, ALU.add, m, a)

        def small_side():
            b = 3
            ps = PS[b]
            for q in range(8):
                xh, xl = XH[:, q, :], XL[:, q, :]
                for j, (l, r) in enumerate(((gswH[:, q, :], xh), (gswL[:, q, :], xh), (gswH[:, q, :], xl))):
                    t = mm(ps[0:24, 0:256], l, r, q == 0 and j == 0, q == 7 and j == 2, xt_tok[q], tk["gsw"],
                           bank_free[b], sig=q == 7 and j == 2)
            yield
            k = dve.do(lambda e: e.tensor_copy(gst[:], ps[0:24, 0:256]), t, tk["b2"])
            yield from pause(2)
            for a in range(2):
                t = pe.do(lambda e, a=a: e.transpose(ps[:, 256 + 24 * a:280 + 24 * a], gst[:, a * P:(a + 1) * P],
                                                     ident[0:24, 0:24]), k)
            yield
            k = dve.do(lambda e: e.tensor_copy(gsm[:], ps[:, 256:304].rearrange("p (a n) -> p a n", a=2)), t)
            bank_free[b] = [k]
            yield
            tmp = stt2[:, 0:2, :]
            x1 = tt(dve, G_g, gsm[:, :, 0:8], mid(hb[:, 0, :], 2), ALU.add, k, hb_in)
            s = softplus(G_G, G_g, tmp, [x1, tk["b2"]])
            ea = afn(hb[:, 1, :], hb[:, 1, :], ACT.Exp, hb_in)
            n = ts(dve, hb[:, 1, :], hb[:, 1, :], -1.0, None, ALU.mult, None, ea)
            g = tt(dve, G_g, G_G, mid(hb[:, 1, :], 2), ALU.mult, s, n)
            tmp2, tmp3 = stt2[:, 2:4, :], stt2[:, 4:6, :]
            s = softplus(tmp3, gsm[:, :, 8:16], tmp2, [k, tk["b2"]], -1.0)
            be = afn(G_beta, tmp3, ACT.Exp, s, scale=-1.0)
            x2 = tt(dve, gsm[:, :, 16:24], gsm[:, :, 16:24], mid(hb[:, 2, :], 2), ALU.add, k, hb_in)
            s = softplus(G_gl, gsm[:, :, 16:24], tmp2, [x2, be], -1.0)
            lf = ts(dve, G_lf, G_gl, -1.0, None, ALU.mult, None, s)
            yield from pause(6)
            b = 4
            ps4 = PS[b]
            mm(ps4[0:8, 0:128], G_lf[:, 0, :], UF[:], True, True, lf, late, bank_free[b], loose=True)
            mm(ps4[0:8, 128:256], G_lf[:, 0, :], ones[:], True, False, loose=True)
            mm(ps4[0:8, 128:256], G_lf[:, 1, :], UF[:], False, True, loose=True)
            mm(ps4[32:40, 0:128], G_lf[:, 0, :], UF[:], True, True, loose=True)
            mm(ps4[32:40, 128:256], G_lf[:, 0, :], ones[:], True, False, loose=True)
            t = mm(ps4[32:40, 128:256], G_lf[:, 1, :], UF[:], False, True, sig=True, loose=True)
            z = setm(CL[:], 0.0, tk["b2"])
            z = setm(CL[0:8, :], 1.0, z)
            z2 = setm(CX[:], 0.0, tk["b2"])
            z2 = setm(CX[32:64, :], 1.0, z2)
            m = setm(HM[:], 0.0, tk["b2"])
            m = sel(HM[0:32, :], ALU.not_equal, 1.0, 0, [[-1, 8]], 1, m)
            tk["HM"] = sel(HM[32:64, :], ALU.not_equal, 1.0, 0, [[-1, 8]], 1, m)
            c1 = dve.do(lambda e: e.tensor_copy(CL[32:40, :], ps4[32:40, 0:256]), t, z)
            c2 = ts(dve, CX[0:8, :], ps4[0:8, 0:256], -1.0, None, ALU.mult, None, t, z2)
            bank_free[b] = [c1, c2]
            tk["CL"], tk["CX"] = c1, c2
            yield
            b = 5
            ps5 = PS[b]
            pe.wait([g, late, bank_free[b]])
            gg = G_g.rearrange("p a h -> p (a h)")
            mm(ps5[:, 0:16], UI[:], gg, True, True, loose=True)
            mm(ps5[:, 16:32], UL[:], gg, True, True, loose=True)
            for c in range(2):
                t = mm(ps5[:, 32 + 16 * c:48 + 16 * c], ONEB[:, c, :], gg, True, True, sig=c == 1, loose=True)
            yield from pause(2)
            v2 = "p (a h) -> p a h"
            k = dve.do(lambda e: e.tensor_copy(G_G, ps5[:, 0:16].rearrange(v2, a=2)), t, g)
            k1 = afn(G_dec, ps5[:, 16:32].rearrange(v2, a=2), ACT.Exp, k)
            k2 = afn(DEC[:].rearrange("p (a c) h -> p c a h", c=2), ps5[:, 32:64].rearrange("p (c a h) -> p c a h", c=2, a=2),
                     ACT.Exp, tk["b2"])
            k0 = afn(G_eG, G_G, ACT.Exp, k)
            bank_free[b] = [k2]
            tk["Gs"] = [k, k0, k1, k2]
            yield from pause(2)
            for a in range(2):
                for h4 in range(2):
                    b = 3 + (2 * a + h4) % 2
                    for j in range(4):
                        h = 4 * h4 + j
                        gcol = G_g[:, a, h:h + 1].broadcast_to([P, P])
                        t = mm(PS[b][:, j * P:(j + 1) * P], gcol, UI[:], True, True, bank_free[b], sig=j == 3)
                    yield
                    for j in range(4):
                        h = 4 * h4 + j
                        k = ts(dve, Ev[:, a, h, :], PS[b][:, j * P:(j + 1) * P], G_G[:, a, h:h + 1], 0.0, ALU.subtract,
                               ALU.min, t, tk["Gs"], tk["fg_free"])
                    bank_free[b] = [k]
                    v = Ev[:, a, 4 * h4:4 * h4 + 4, :]
                    k = afn(v, v, ACT.Exp, k)
                    tk["E", a, h4] = tt(pool, v, v, mid(UI[:], 4), ALU.mult, k)
                    yield from pause(2)
            tk["E_all"] = tk["small"] = True

        def bcast(col2, bank, toks):
            for a in range(2):
                t = mm(PS[bank][:, a * P:(a + 1) * P], col2(a).broadcast_to([P, P]), ident[:], True, True, toks,
                       bank_free[bank], sig=a == 1)
            return t

        def fox_norm(key, i, tm, dst, k, sums, rstd, post):
            b = 6 + i % 2
            v = tm[:, :, 256 * i:256 * i + 256].rearrange("p a (j d) -> p a j d", j=2)
            js = jk[i % 2][:].rearrange("p (a j d) -> p a j d", a=2, j=2)
            hs = slice(2 * i, 2 * i + 2)
            k1 = afn(js, v, ACT.Square, k, tk["b2"], tk.get(("jk", i % 2)))
            yield from pause(2)
            r = dve.do(lambda e: e.tensor_reduce(sums[:, :, hs], js, AX, ALU.add), k1)
            tk["jk", i % 2] = r
            r = ts(pool, sums[:, :, hs], sums[:, :, hs], 1.0 / 128, 1e-6, ALU.mult, ALU.add, r)
            r = tt(pool, rstd[:, :, hs], sums[:, :, hs], npow[:, 0:4].rearrange("p (a h) -> p a h", a=2), ALU.pow, r)
            if post != 1.0:
                r = ts(pool, rstd[:, :, hs], rstd[:, :, hs], post, None, ALU.mult, None, r)
            yield from pause(5)
            r = [tt(dve, v[:, a], v[:, a], last(rstd[:, a, hs], P), ALU.mult, r, k1) for a in range(2)]
            yield from pause(5)
            for j in range(2):
                for a in range(2):
                    t = tr(PS[b][:, (2 * j + a) * P:(2 * j + a + 1) * P], v[:, a, j, :], r, bank_free[b],
                           sig=j == 1 and a == 1)
            yield
            if key == "fk":
                while ("fq", 3) not in tk:
                    yield
            kk = afn(dst[:, hs], PS[b][:].rearrange("p (j a d) -> p j a d", j=2, a=2) if key == "fk" else
                     PS[b][:].rearrange("p (j t) -> p j t", j=2), ACT.Identity, t, tk.get(("fq", 3)) if key == "fk" else (),
                     scale=COLS[:, CG[key]:CG[key] + 1])
            bank_free[b] = [kk]
            tk[key, i] = [kk, t]

        def fqk_evac(tm, dst, key, i, sums, rstd, post):
            def evac(ps, t):
                k = afn(tm[:, :, 256 * i:256 * i + 256], ps[:].rearrange("p (a n) -> p a n", a=2), ACT.Copy, t, tk["b2"])
                side.append(fox_norm(key, i, tm, dst, k, sums, rstd, post))
                return [k]
            return evac

        fox_left = [2]

        def fox_attention(e_):
            b = 3 + e_
            S, O, s, sTe = PS[b], PS[5 + e_], sS[e_], sT[e_]
            halves = ((0, 128), (128, 384))
            m0 = stt2[:, 6, 2 * e_:2 * e_ + 2]
            l0 = stt2[:, 7, 2 * e_:2 * e_ + 2]
            t_s = t_o = None
            while not all(("fk", n) in tk for n in range(4)) or "CX" not in tk or "small" not in tk:
                yield

            def bias(h):
                return tt(pool, CR[e_][:], CX[:], HM[:, h:h + 1].broadcast_to([64, T]), ALU.mult, tk["CX"], tk["HM"], t_s)

            cr = bias(e_)
            yield from pause(2)
            for h in range(e_, NH, 2):
                pe.wait([tk["fq", h // 2], tk["fk", h // 2], bank_free[b], tk["CL"]])
                mm(S[:, 0:128], fqT[:, h, 0:128], fkT[:, h, 0, :], True, False, loose=True)
                mm(S[:, 0:128], CL[:, 0:128], CR[e_][:, 0:128], False, True, cr, loose=True)
                mm(S[:, 128:384].rearrange("p (a d) -> p a d", a=2), fqT[:, h, 128:256], fkT[:, h], True, False, loose=True)
                t_s = mm(S[:, 128:384], CL[:, 128:256], CR[e_][:], False, True, sig=True, loose=True)
                if h + 2 < NH:
                    cr = bias(h + 2)
                yield from pause(2)
                k = tt(dve, s[:], S[:, 0:384], MK3[:], ALU.add, t_s)
                rs_ = [dve.do(lambda e, n=n, u=u, v=v: e.tensor_reduce(m0[:, n:n + 1], s[:, u:v], AX, ALU.max, negate=True),
                              k) for n, (u, v) in enumerate(halves)]
                ks = [afn(s[:, u:v], s[:, u:v], ACT.Exp, rs_, bias=m0[:, n:n + 1], accum_out=l0[:, n:n + 1])
                      for n, (u, v) in enumerate(halves)]
                yield from pause(5)
                r = dve.do(lambda e: e.reciprocal(l0, l0), ks)
                ns = [afn(s[:, u:v], s[:, u:v], ACT.Identity, r, scale=l0[:, n:n + 1])
                      for n, (u, v) in enumerate(halves)]
                yield from pause(8)
                for n in range(3):
                    t = tr(S[:, n * P:(n + 1) * P], s[:, n * P:(n + 1) * P], ns, k, sig=n == 2)
                yield
                k = afn(sTe[:], S[:, 0:384], ACT.Copy, t, t_o)
                bank_free[b] = [k]
                yield from pause(3)
                while ("fv", h // 2) not in tk:
                    yield
                mm(O[:, 0:256], fvm[:, 0, h * P:(h + 1) * P], sTe[:, 0:256], True, False, k, tk["fv", h // 2],
                   bank_free[5 + e_], loose=True)
                t_o = mm(O[:, 128:256], fvm[:, 1, h * P:(h + 1) * P], sTe[:, 256:384], False, True, sig=True, loose=True)
                yield
                hh = afn(obH[:, h, :], O[:, 0:256], ACT.Copy, t_o, tk["b2"])
                yield from pause(2)
                ll = tt(dve, obL[:, h, :], O[:, 0:256], obH[:, h, :].bitcast(F32), ALU.subtract, hh, tk["b2"])
                bank_free[5 + e_] = [ll]
                tk["ob", h] = [hh, ll]
            fox_left[0] -= 1
            if fox_left[0] == 0:
                tk["fox"] = fence()

        for i in range(4):
            unit(w_cols(w2, 0, 8, FQ + 256 * i), 8, "A", XH, XL, xt_of,
                 fqk_evac(fqm, fqT, "fq", i, G_sq, G_D, 128 ** -0.5), before=third_norm if i == 0 else None, fresh=i == 0)
        for i in range(4):
            unit(w_cols(w2, 0, 8, FK + 256 * i), 8, "A", XH, XL, xt_of,
                 fqk_evac(fkm, fkT, "fk", i, G_sk, G_Dd, 1.0))
        for i in range(4):
            def fv_evac(ps, t, i=i):
                k = afn(fvm[:, :, 256 * i:256 * i + 256], ps[:].rearrange("p (a n) -> p a n", a=2), ACT.Copy, t, tk["b2"])
                tk["fv", i] = k
                return [k]
            unit(w_cols(w2, 0, 8, FV + 256 * i), 8, "A", XH, XL, xt_of, fv_evac,
                 before=(lambda: side.extend([fox_attention(0), fox_attention(1), decay_rows()])) if i == 0 else None)

        def conv4_evac(dst, n, i):
            sl = dst[:, 2 * i:2 * i + 2, :]

            def fin(done):
                tk["cv", n, i] = done
                if n and i == 3:
                    defer(3, silu_k_and_q if n == 1 else silu_v)
            return lambda ps, t: conv_evac(sl, CG["gdn"], 24, 4, 8 * (1, 0, 2)[n] + 2 * i, ("x", 0), fin)(
                ps, [t, tk["b2"], tk["jk", 0], tk["jk", 1]])

        def silu(dst, n):
            tk["silu", n] = afn(dst[:], dst[:], ACT.Silu, [tk["cv", n, i] for i in range(4)])

        def silu_k_and_q():
            silu(gk, 0)
            silu(gq, 1)
            side.append(q_decay())
            side.extend(prologue(a, g) for a in range(2) for g in range(2))

        def silu_v():
            silu(gv, 2)

        for n, dst in enumerate((gk, gq, gv)):
            for i in range(4):
                unit(w_cols(w2, 0, 8, (GK, GQ, GV)[n] + 256 * i), 8, "B", XH, XL, xt_of, conv4_evac(dst, n, i))

        kb = reg("kb", [P, 8, T], 24)
        qd = reg("qd", [P, 8, T], 32)
        tA = [[reg(f"tA{n}{i}", [P, 4, P], 40 + 2 * (3 * i + n)) for n in range(3)] for i in range(3)]
        GPv = GP[:].rearrange("p (n h t) -> p n h t", n=2, h=4)
        tA.append([reg("tA03", [P, 4, P], 58)[:], GPv[:, 0], GPv[:, 1]])
        gz = reg("gz", [P, 8, T], 60)
        sg2 = reg("sg2", [P, 8, T], 68)
        mb = XS
        mbv = mb[:].rearrange("p a (c t) -> p (a c) t", t=T)
        S0 = reg("S0", [P, 8, P], 40)
        S1 = reg("S1", [P, 8, P], 44)
        Sd = reg("Sd", [P, 8, P], 48)
        VN = reg("VN", [P, 8, P], 52)
        oS = FG
        oSv = oS[:].rearrange("p a (h d) -> p a h d", h=8)
        oaH = reg("oaH", [P, 8, T], 24, F32R)
        oaL = reg("oaL", [P, 8, T], 32, F32R)
        mH = reg("mH", [P, 8, T], 0, F32R)
        mL = reg("mL", [P, 8, T], 8, F32R)
        sgb = [reg(f"sgb{i}", [P, 2, T], 76 + 2 * i) for i in range(2)]
        tokP = {}
        chains_left = [4]

        def decay_rows():
            while not all(("fk", n) in tk for n in range(4)) or "small" not in tk:
                yield
            b = 7
            for h in range(NH):
                t = bcast(lambda a: G_eG[:, a, h:h + 1], b, tk["Gs"])
                yield from pause(2)
                bank_free[b] = [afn(qd[:, h, :], PS[b][:, 0:256], ACT.Copy, t, [tk["fk", n] for n in range(4)])]
                tokP["eG", h] = bank_free[b]
                yield from pause(2)

        def q_decay():
            for i in range(4):
                hs = slice(2 * i, 2 * i + 2)
                r = tt(pool, qd[:, hs, :], qd[:, hs, :], gq[:, hs, :], ALU.mult, tokP["eG", 2 * i], tokP["eG", 2 * i + 1],
                       tk["silu", 1])
                tokP["qd", 2 * i] = tokP["qd", 2 * i + 1] = r
                yield from pause(2)

        def prologue(a, g):
            hs = range(4 * g, 4 * g + 4)
            AT, Y, Tm = tA[2 * a + g]
            AT, Y, Tm = AT[:, :, :], Y[:, :, :], Tm[:, :, :]
            b = 3 + 2 * a + g
            B4 = PS[b][:].rearrange("p (h t) -> p h t", h=4)
            tk_ = slice(a * P, (a + 1) * P)
            hsl = slice(4 * g, 4 * g + 4)
            Eg = Ev[:, a, hsl, :]
            kbs, gqs, gks, gvs = (v[:, hsl, tk_] for v in (kb, gq, gk, gv))

            def each(f, *toks):
                for j, h in enumerate(hs):
                    t = f(PS[b][:, j * P:(j + 1) * P], j, h, *toks, sig=j == 3)
                return t

            def turn(src, *toks):
                return each(lambda o, j, h, *tt_, sig: tr(o, src(j, h), *tt_, sig=sig), *toks)

            def prod(l, r, *toks):
                return each(lambda o, j, h, *tt_, sig: mm(o, l(j, h), r(j, h), True, True, *tt_, sig=sig), *toks)

            while "fox" not in tk or "E_all" not in tk:
                yield
            f0 = [tk["fox"], tk["E", a, g], tk["Gs"]]
            yield from pause(6 + 10 * a + 3 * g)
            t = turn(lambda j, h: gk[:, h, tk_], tk["silu", 0], f0, bank_free[b])
            yield
            kC = act.do(lambda e: e.activation(kbs, B4, ACT.Copy), t, f0)
            kS = act.do(lambda e: e.activation(Tm, kbs, ACT.Square), kC)
            yield
            t = turn(lambda j, h: gq[:, h, tk_], tk["silu", 1], kC)
            yield
            kQ = act.do(lambda e: e.activation(Y, B4, ACT.Square), t)
            yield
            sk, D_, Dd, rt = (v[:, a, hsl] for v in (G_sk, G_D, G_Dd, G_rt))
            r1 = dve.do(lambda e: e.tensor_reduce(sk, Tm, AX, ALU.add), kS)
            k = ts(dve, sk, sk, 1e-6, None, ALU.add, None, r1)
            kr = tt(pool, rt, sk, ppow[:], ALU.pow, k, late)
            kD = dve.do(lambda e: e.reciprocal(D_, sk), k)
            kD = tt(dve, D_, D_, G_beta[:, a, hsl], ALU.mult, kD)
            kDd = tt(dve, Dd, D_, G_dec[:, a, hsl], ALU.mult, kD)
            t = prod(lambda j, h: gk[:, h, tk_], lambda j, h: gk[:, h, tk_], kQ)
            yield
            rq = dve.do(lambda e: e.tensor_reduce(G_sq[:, a, hsl], Y, AX, ALU.add), kQ)
            tokP["sq", a, g] = rq
            yield from pause(4)
            kA = [stt(AT[:, j], B4[:, j], D_[:, j:j + 1], Eg[:, j], ALU.mult, ALU.mult, t, kD, f0) for j in range(4)]
            kY = tt(pool, Y, AT, mid(M1T[:], 4), ALU.mult, kA, rq, late)
            kY = tt(pool, Y, Y, mid(ident[:], 4), ALU.add, kY)
            yield from pause(6)
            t = prod(lambda j, h: gk[:, h, tk_], lambda j, h: gq[:, h, tk_], kA)
            yield from pause(2)
            while not all(("qd", h) in tokP for h in hs):
                yield
            kT_ = [stt(gqs[:, j], B4[:, j], D_[:, j:j + 1], Eg[:, j], ALU.mult, ALU.mult, t, tokP["qd", h])
                   for j, h in enumerate(hs)]
            tokP["att", a, g] = kT_
            yield
            if ("silu", 2) not in tk:
                while ("silu", 2) not in tk:
                    yield
                yield from pause(4)
            t = turn(lambda j, h: gv[:, h, tk_], kT_, tk["silu", 2])
            yield from pause(2)
            rv = tt(dve, gvs, B4, last(rt, P), ALU.mult, t, kr)
            yield
            for i in range(5):
                t = turn(lambda j, h: Y[:, j, :], kY, rv)
                yield
                kTm = act.do(lambda e: e.activation(Tm, B4, ACT.Copy), t, r1)
                yield
                t = prod(lambda j, h: AT[:, j, :], lambda j, h: Tm[:, j, :], kTm)
                yield
                kU = tt(dve, Tm, B4, mid(ML[:, i, :], 4), ALU.mult, t)
                yield
                tY = prod(lambda j, h: Tm[:, j, :], lambda j, h: Y[:, j, :], kU)
                yield
                kY = tt(dve, Y, Y, B4, ALU.add, tY)
                rv = kY
                yield
            kR = tt(dve, Tm, kbs, last(G_eG[:, a, hsl], P), ALU.mult, tY, kC)
            kd = tt(pool, kbs, kbs, last(Dd, P), ALU.mult, kDd, kR)
            tokP["kd", a, g] = kd
            t = prod(lambda j, h: Y[:, j, :], lambda j, h: gv[:, h, tk_], kY)
            yield
            kV = act.do(lambda e: e.activation(gvs, B4, ACT.Copy), t)
            yield
            t = prod(lambda j, h: Tm[:, j, :], lambda j, h: Y[:, j, :], kR, kV)
            yield
            kC = act.do(lambda e: e.activation(gks, B4, ACT.Copy), t)
            bank_free[b] = [kC]
            tokP["v", a, g], tokP["c", a, g] = kV, kC
            tokP["end", a, g] = [kV, kC, t, kd]
            chains_left[0] -= 1
            if chains_left[0] == 0:
                side.append(scan())

        def scan():
            ends = [tokP["end", a, g] for a in range(2) for g in range(2)]
            Scur, Snxt = S0, S1
            kS = [None, None]
            st = {}
            for c in range(4):
                a, o = c // 2, 64 * (c % 2)
                rows_ = slice(o, o + 64)
                cols_ = slice(a * P + o, a * P + o + 64)
                vn = VN[rows_] if c else gv[rows_, :, 0:P]
                for g in range(2):
                    if c == 0:
                        st["kv", g] = ends
                        pe.wait([bank_free[5 + g]])
                        continue
                    hs = range(4 * g, 4 * g + 4)
                    hsl = slice(4 * g, 4 * g + 4)
                    bP, bQ = 3 + g, 5 + g
                    for j, h in enumerate(hs):
                        t = mm(PS[bP][rows_, j * P:(j + 1) * P], gk[:, h, cols_], Scur[:, h, :], True, True, kS[g],
                               tokP["c", a, g], bank_free[bP], sig=j == 3, loose=True)
                    for j, h in enumerate(hs):
                        mm(PS[bQ][rows_, j * P:(j + 1) * P], qd[:, h, cols_], Scur[:, h, :], j == 0, False, bank_free[bQ],
                           loose=True)
                    kv = tt(dve, VN[rows_, hsl, :], gv[rows_, hsl, a * P:(a + 1) * P],
                            PS[bP][rows_, :].rearrange("p (h d) -> p h d", h=4), ALU.subtract, t, tokP["v", a, g],
                            st.get(("vn", g)), ends)
                    bank_free[bP] = [kv]
                    if c < 3:
                        st["sd", g] = tt(pool, Sd[:, hsl, :], Scur[:, hsl, :], last(DEC[:, c, hsl], P), ALU.mult, kS[g],
                                         st.get(("sn", g)), ends)
                    st["kv", g] = kv
                    yield
                yield
                for g in range(2):
                    hs = range(4 * g, 4 * g + 4)
                    hsl = slice(4 * g, 4 * g + 4)
                    bQ, bS = 5 + g, 3 + g
                    pe.wait([st["kv", g], tokP["att", a, g], tokP["kd", a, g]])
                    if c < 3:
                        for j, h in enumerate(hs):
                            t = mm(PS[bS][:, j * P:(j + 1) * P], kb[rows_, h, a * P:(a + 1) * P], vn[:, h, :], True, True,
                                   bank_free[bS], sig=j == 3, loose=True)
                        news = PS[bS][:].rearrange("p (h d) -> p h d", h=4)
                        if c:
                            kS[g] = tt(dve, Snxt[:, hsl, :], Sd[:, hsl, :], news, ALU.add, t, st["sd", g], st.get(("r", g)))
                        else:
                            kS[g] = afn(Snxt[:, hsl, :], news, ACT.Copy, t, ends)
                        st["sn", g] = kS[g]
                        bank_free[bS] = [kS[g]]
                    for j, h in enumerate(hs):
                        t = mm(PS[bQ][rows_, j * P:(j + 1) * P], gq[rows_, h, cols_], vn[:, h, :], c == 0 and j == 0, j == 3,
                               sig=j == 3, loose=True)
                    st["vn", g] = t
                    st["r", g] = t
                    k = afn(oSv[rows_, a, hsl, :], PS[bQ][rows_, :].rearrange("p (h d) -> p h d", h=4), ACT.Copy, t, ends)
                    bank_free[bQ] = [k]
                    tokP["o", c, g] = k
                    yield
                Scur, Snxt = Snxt, Scur
                if c % 2:
                    side.append(o_norm(a))

        def o_norm(a):
            al = [tokP["o", c, g] for c in (2 * a, 2 * a + 1) for g in range(2)] + [pe.now()]
            sq = kb[:, :, a * P:(a + 1) * P]
            yield from pause(2)
            k = afn(sq, oSv[:, a, :, :], ACT.Square, al)
            yield from pause(2)
            os_, fa, s2 = G_os[:, a, :], G_fac[:, a, :], G_sq[:, a, :]
            k = dve.do(lambda e: e.tensor_reduce(os_, sq, AX, ALU.add), k)
            k2 = ts(dve, s2, s2, 1e-6, 128e-6, ALU.add, ALU.mult, tokP["sq", a, 0], tokP["sq", a, 1])
            k = stt(os_, os_, 1.0 / 128, s2, ALU.mult, ALU.add, k, k2)
            k = tt(pool, fa, os_, npow[:, 0:8], ALU.pow, k)
            yield from pause(4)
            tokP["sc", a] = tt(dve, oSv[:, a, :, :], oSv[:, a, :, :], last(fa, P), ALU.mult, k)
            if a == 1:
                side.append(o_turn())

        def o_turn():
            sc = [tokP["sc", a] for a in range(2)]
            st = {}
            tmps = VN[:].rearrange("p h d -> p (h d)")
            while ("gz", 3) not in tk:
                yield
            for i in range(4):
                b = 3 + i
                for j in range(2):
                    for a in range(2):
                        h = 2 * i + j
                        t = tr(PS[b][:, j * 256 + a * P:j * 256 + (a + 1) * P], oSv[:, a, h, :], sc, bank_free[b],
                               sig=j == 1 and a == 1)
                st[i] = t
            for i in range(4):
                b = 3 + i
                tmp = tmps[:, (i % 2) * 512:(i % 2) * 512 + 512]
                zz = gz[:, 2 * i:2 * i + 2, :].rearrange("p c t -> p (c t)")
                k = stt(tmp, PS[b][:], COLS[:, CG["gn"]:CG["gn"] + 1], zz, ALU.mult, ALU.mult, st[i], tk["gz", i],
                        st.get(("oa", i - 2)))
                bank_free[b] = [k]
                yield from pause(2)
                s = split(oaH[:, 2 * i:2 * i + 2, :].rearrange("p c t -> p (c t)"),
                          oaL[:, 2 * i:2 * i + 2, :].rearrange("p c t -> p (c t)"), tmp, [k], sc)
                st["oa", i] = s
                tk["oa", 2 * i] = tk["oa", 2 * i + 1] = s
                yield

        def ob_of(q):
            return tk.get(("ob", q))

        def yb_evac(i):
            def evac(ps, t):
                k = tt(dve, mbv[:, 2 * i:2 * i + 2, :].rearrange("p c t -> p (c t)"), ps[:],
                       sgb[i % 2][:].rearrange("p c t -> p (c t)"), ALU.mult, t, tk["gb", i], tk["mbf"])
                tk["free", "gb", i + 2] = k
                tk["mb", i] = k
                return [k]
            return evac

        def fox_end():
            while "fox" not in tk:
                tick()
            for i in range(2):
                tk["free", "gb", i] = tk["fox"]
            tk["mbf"] = tk["fox"]

        for i in range(4):
            unit(w_cols(w2, 0, 8, GTB + 256 * i), 8, "B", XH, XL, xt_of, gate_evac(sgb[i % 2][:], "gb", i),
                 before=fox_end if i == 0 else None)
            unit(w_cols(w_proj_fox_2[0], 0, 8, 256 * i), 8, "B", obH, obL, ob_of, yb_evac(i))

        def ob_done():
            for i in range(4):
                tk["free", "gz", i] = tk["free", "ga2", i] = pe.now()

        for i in range(4):
            unit(w_cols(w2, 0, 8, GZ + 256 * i), 8, "B", XH, XL, xt_of,
                 gate_evac(gz[:, 2 * i:2 * i + 2, :], "gz", i, ACT.Silu), before=ob_done if i == 0 else None)
        for i in range(4):
            unit(w_cols(w2, 0, 8, GTA + 256 * i), 8, "B", XH, XL, xt_of, gate_evac(sg2[:, 2 * i:2 * i + 2, :], "ga2", i))

        def oa_of(q):
            return tk.get(("oa", q))

        m2_tok = [None] * 8

        def end_gdn():
            drain()
            tk["gdn_end"] = fence()

        def ya_evac(i):
            def evac(ps, t):
                sl = slice(2 * i, 2 * i + 2)
                v = sg2[:, sl, :]
                k = tt(dve, v.rearrange("p c t -> p (c t)"), ps[:], v.rearrange("p c t -> p (c t)"), ALU.mult, t,
                       tk["ga2", i])
                k2 = tt(dve, v, v, mbv[:, sl, :], ALU.add, k, tk["mb", i])

                def got(r):
                    m2_tok[2 * i] = m2_tok[2 * i + 1] = tk["m2"] = r
                split_later(mH[:, sl, :], mL[:, sl, :], v, [k2], tk["gdn_end"], got, i == 3)
                return [k]
            return evac

        for i in range(4):
            unit(w_cols(w_proj_gdn_2[0], 0, 8, 256 * i), 8, "B", oaH, oaL, oa_of, ya_evac(i),
                 before=end_gdn if i == 0 else None)

        def m2_of(q):
            return m2_tok[q]

        res = {}

        def wo2_evac(i):
            def evac(ps, t, a):
                v = XRES[:, a, 256 * i:256 * i + 256]
                k = res[a, i] = tt(dve, v, v, ps, ALU.add, t)
                if i == 3:
                    xs_free["t"] = [tk["m2"], pool.now()]
                    tk["q", a] = squares(a, [res[a, n] for n in range(4)])
                    scaled(a, rstd(a, a, tk["q", a]), tk["q", a])
                return [k]
            return evac

        for i in range(4):
            unit(w_cols(w_out_2[0], 0, 8, 256 * i), 8, "A", mH, mL, m2_of, wo2_evac(i), halves=True, fresh=i == 0)

        f2H = reg("f2H", [P, FC2, T], 0, F32R)
        f2L = reg("f2L", [P, FC2, T], 32, F32R)
        rr = [reg(f"rr{i}", [P, 2, T], 64 + 2 * i) for i in range(3)]
        f2_tok = [None] * FC2

        def fourth_norm():
            xt_read["t"] = [pe.now()]
            keep_warm(WARM[0])
            norm_to_xt(CG["mlp2"])
            tk["f2"] = fence()

        def up2_evac(i):
            def evac(ps, t):
                r = rr[i % 3]
                k = afn(r[:].rearrange("p c t -> p (c t)"), ps[:], ACT.Relu, t, tk.get(("rr", i - 3)), tk["f2"])
                k2 = afn(f2H[:, 2 * i:2 * i + 2, :], r[:], ACT.Square, k, tk["f2"])
                k3 = tt(pool, r[:], r[:], r[:], ALU.mult, k2)

                def rest():
                    l = tt(dve, f2L[:, 2 * i:2 * i + 2, :], r[:], f2H[:, 2 * i:2 * i + 2, :].bitcast(F32), ALU.subtract,
                           k2, k3, tk["f2"])
                    tk["rr", i] = l
                    f2_tok[2 * i] = f2_tok[2 * i + 1] = [k2, l]
                defer(4, rest)
                return [k]
            return evac

        for i in range(FC2 // 2):
            unit(w_cols(w_up_2[0], 0, 8, 256 * i), 8, "B", XH, XL, xt_of, up2_evac(i),
                 before=fourth_norm if i == 0 else None, fresh=i == 0)

        def f2_of(q):
            return f2_tok[q]

        outs = []
        ov = out[0].rearrange("(a p) n -> p a n", p=P)
        s_out = sem("s_out")

        def fin_evac(i):
            def evac(ps, t, a):
                v = XRES[:, a, 256 * i:256 * i + 256]
                k = tt(dve, v, v, ps, ALU.add, t)
                outs.append((a, i, k))
                return [k]
            return evac

        for i in range(4):
            for n in range(4):
                unit(w_cols(w_down_2[0], n * 8 * P, 8, 256 * i), 8, "A", f2H, f2L, f2_of, fin_evac(i), k0=8 * n, halves=True,
                     first=n == 0, last_=n == 3)

        run_units()
        for a, i, k in outs:
            sp.wait([k])
            sp.prog.append(lambda e, a=a, i=i: e.dma_start(ov[:, a, 256 * i:256 * i + 256],
                                                           XRES[:, a, 256 * i:256 * i + 256]).then_inc(s_out, 16))
        sp.prog.append(lambda e: e.wait_ge(s_out, 128))

        block = ctx.enter_context(nc.Block())
        for q, name in ((sp, "sync"), (act, "scalar"), (dve, "vector"), (pool, "gpsimd"), (pe, "tensor")):
            def body(e, q=q):
                q.play(e)
            {"sync": block.sync, "scalar": block.scalar, "vector": block.vector, "gpsimd": block.gpsimd,
             "tensor": block.tensor}[name](body)


_INS = ["x", "norm_mix_pre", "w_in", "conv_mix_w", "w_att_branch", "w_conv_branch", "w_out", "norm_mix_post",
        "norm_ffn_pre", "w_up", "conv_ffn_w", "w_down", "norm_ffn_post", "norm_mix_g_2", "w_in_2", "gdn_conv_w_2",
        "gdn_a_log_2", "gdn_dt_bias_2", "gdn_norm_g_2", "fox_q_norm_g_2", "fox_k_norm_g_2", "fox_f_bias_2",
        "w_proj_gdn_2", "w_proj_fox_2", "w_out_2", "norm_mlp_g_2", "w_up_2", "w_down_2"]


def kernel(**inputs):
    import numpy as _np
    import concourse.bacc as _bacc
    from concourse.bass_utils import run_bass_kernel_spmd as _run

    nc = _bacc.Bacc("TRN2", target_bir_lowering=False, num_devices=1)
    arrays, args = {}, []
    for name in _INS:
        a = _np.ascontiguousarray(inputs[name])
        arrays[f"in_{name}"] = a
        args.append(nc.dram_tensor(f"in_{name}", a.shape, mybir.dt.from_np(a.dtype), kind="ExternalInput").ap())
    args.append(nc.dram_tensor("out_0", (1, T, D), F32, kind="ExternalOutput").ap())
    two_blocks(nc, *args)
    r = _run(nc, [arrays], core_ids=[0])
    return r.results[0]["out_0"]
```
